# Optimizing a Trainium2 kernel written in Bass

```python
import math
import jax, jax.numpy as jnp
from jax import lax
import numpy as np

D_MODEL = 1024
BATCH = 1
SEQ = 1024
DEPTH = 2
DEC_BATCH = 8
DEC_SEQ = 1
PAST_LEN = 1024
PAGE_SIZE = 128

N_A = DEPTH // 2
N_B = DEPTH - N_A
M_HEADS = 4
M_DK = 128
M_DV = 256
M_CHUNK = 64
M_IN = 2 * M_HEADS * M_DK + 2 * M_HEADS * M_DV + 2 * M_HEADS
D_FF = 2816
CONV_W = 3
MLA_HEADS = 16
Q_LORA = 384
KV_LORA = 256
QK_NOPE = 64
QK_ROPE = 32
V_HEAD = 64
ROPE_THETA = 10000.0
Q_BLOCK = 128
ATT_SCALE = (QK_NOPE + QK_ROPE) ** -0.5
EPS = 1e-6

kernel_name = 'yoco_mlstm_mla_convffn_adaln_step'

def rms_norm(x, g):
    xf = x.astype(jnp.float32)
    y = xf * lax.rsqrt(jnp.mean(xf * xf, axis=-1, keepdims=True) + EPS)
    return (y * g.astype(jnp.float32)).astype(x.dtype)

def ada_mod(c, w, b, n):
    mod = jax.nn.silu(c) @ w + b
    return jnp.split(mod[:, None, :], n, axis=-1)

def apply_rope(x, pos):
    half = x.shape[-1] // 2
    freq = ROPE_THETA ** (-jnp.arange(half, dtype=jnp.float32) / half)
    ang = pos.astype(jnp.float32)[:, None] * freq[None, :]
    cos = jnp.cos(ang)[None, :, None, :]
    sin = jnp.sin(ang)[None, :, None, :]
    xf = x.astype(jnp.float32)
    x1, x2 = xf[..., :half], xf[..., half:]
    return jnp.concatenate([x1 * cos - x2 * sin, x1 * sin + x2 * cos], axis=-1).astype(x.dtype)

def mlstm_chunkwise(q, k, v, log_i, log_f):
    bsz, nh, s, _ = q.shape
    nc = s // M_CHUNK
    qc = q.reshape(bsz, nh, nc, M_CHUNK, M_DK)
    kc = k.reshape(bsz, nh, nc, M_CHUNK, M_DK)
    vc = v.reshape(bsz, nh, nc, M_CHUNK, M_DV)
    li = log_i.reshape(bsz, nh, nc, M_CHUNK)
    b = jnp.cumsum(log_f.reshape(bsz, nh, nc, M_CHUNK), axis=-1)
    g = b[..., -1]
    a = g[..., None] - b + li
    m_loc = jnp.max(a, axis=-1)
    wa = jnp.exp(a - m_loc[..., None])
    c_loc = jnp.einsum('bhcld,bhcle->bhcde', kc * wa[..., None], vc)
    n_loc = jnp.einsum('bhcl,bhcld->bhcd', wa, kc)

    def chunk_step(carry, inp):
        c_st, n_st, m_st = carry
        g_c, m_l, c_l, n_l = inp
        m_new = jnp.maximum(g_c + m_st, m_l)
        fw = jnp.exp(g_c + m_st - m_new)
        lw = jnp.exp(m_l - m_new)
        c_new = fw[..., None, None] * c_st + lw[..., None, None] * c_l
        n_new = fw[..., None] * n_st + lw[..., None] * n_l
        return (c_new, n_new, m_new), (c_st, n_st, m_st)

    init = (jnp.zeros((bsz, nh, M_DK, M_DV), jnp.float32),
            jnp.zeros((bsz, nh, M_DK), jnp.float32),
            jnp.zeros((bsz, nh), jnp.float32))
    xs = (jnp.moveaxis(g, 2, 0), jnp.moveaxis(m_loc, 2, 0),
          jnp.moveaxis(c_loc, 2, 0), jnp.moveaxis(n_loc, 2, 0))
    final, (c_prev, n_prev, m_prev) = lax.scan(chunk_step, init, xs)
    c_prev = jnp.moveaxis(c_prev, 0, 2)
    n_prev = jnp.moveaxis(n_prev, 0, 2)
    m_prev = jnp.moveaxis(m_prev, 0, 2)
    w0 = b + m_prev[..., None]
    causal = jnp.tril(jnp.ones((M_CHUNK, M_CHUNK), bool))
    dmat = jnp.where(causal, b[..., :, None] - b[..., None, :] + li[..., None, :], -jnp.inf)
    m_s = jnp.maximum(w0, jnp.max(dmat, axis=-1))
    w_inter = jnp.exp(w0 - m_s)
    s_qk = jnp.einsum('bhcid,bhcjd->bhcij', qc, kc) * jnp.exp(dmat - m_s[..., None])
    num = (w_inter[..., None] * jnp.einsum('bhcid,bhcde->bhcie', qc, c_prev)
           + jnp.einsum('bhcij,bhcje->bhcie', s_qk, vc))
    den = w_inter * jnp.einsum('bhcid,bhcd->bhci', qc, n_prev) + jnp.sum(s_qk, axis=-1)
    h = num / jnp.maximum(jnp.abs(den), jnp.exp(-m_s))[..., None]
    return h.reshape(bsz, nh, s, M_DV), final

def mlstm_step(carry, inp):
    c_st, n_st, m_st = carry
    q, k, v, li, lf = inp
    m_new = jnp.maximum(lf + m_st, li)
    fw = jnp.exp(lf + m_st - m_new)
    iw = jnp.exp(li - m_new)
    c_new = fw[..., None, None] * c_st + iw[..., None, None] * (k[..., :, None] * v[..., None, :])
    n_new = fw[..., None] * n_st + iw[..., None] * k
    num = jnp.einsum('bhd,bhde->bhe', q, c_new)
    den = jnp.einsum('bhd,bhd->bh', q, n_new)
    h = num / jnp.maximum(jnp.abs(den), jnp.exp(-m_new))[..., None]
    return (c_new, n_new, m_new), h

def mlstm_recurrent(q, k, v, log_i, log_f, state):
    init = tuple(s_.astype(jnp.float32) for s_ in state)
    xs = (jnp.moveaxis(q, 2, 0), jnp.moveaxis(k, 2, 0), jnp.moveaxis(v, 2, 0),
          jnp.moveaxis(log_i, 2, 0), jnp.moveaxis(log_f, 2, 0))
    final, hs = lax.scan(mlstm_step, init, xs)
    return jnp.moveaxis(hs, 0, 2), final

def mlstm_mixer(h, w_in, b_gates, g_head, w_out, state):
    bsz, s, _ = h.shape
    qd, vd = M_HEADS * M_DK, M_HEADS * M_DV
    proj = h @ w_in
    q, k, v, o, gates = jnp.split(proj, [qd, 2 * qd, 2 * qd + vd, 2 * qd + 2 * vd], axis=-1)

    def heads(t, d):
        return t.reshape(bsz, s, M_HEADS, d).transpose(0, 2, 1, 3).astype(jnp.float32)

    q = heads(q, M_DK) * (M_DK ** -0.5)
    k = heads(k, M_DK)
    v = heads(v, M_DV)
    gates = (gates + b_gates).astype(jnp.float32).transpose(0, 2, 1)
    log_i = gates[:, :M_HEADS]
    log_f = jax.nn.log_sigmoid(gates[:, M_HEADS:])
    if state is None:
        hh, new_state = mlstm_chunkwise(q, k, v, log_i, log_f)
    else:
        hh, new_state = mlstm_recurrent(q, k, v, log_i, log_f, state)
    hh = rms_norm(hh.transpose(0, 2, 1, 3), g_head)
    hh = hh.reshape(bsz, s, vd).astype(h.dtype) * jax.nn.sigmoid(o)
    return hh @ w_out, new_state

def conv_ffn(h, buf, w_up, w_conv, b_conv, w_down):
    s = h.shape[1]
    a, gt = jnp.split(h @ w_up, 2, axis=-1)
    ext = jnp.concatenate([buf.astype(a.dtype), a], axis=1)
    conv = b_conv
    for j in range(CONV_W):
        conv = conv + ext[:, j:j + s] * w_conv[j]
    out = (jax.nn.silu(conv) * gt) @ w_down
    return out, ext[:, -(CONV_W - 1):]

def shared_latent(x, c, pos, g_kv_in, w_ada_kv, b_ada_kv, w_dkv, g_kv):
    shift, scale = ada_mod(c, w_ada_kv, b_ada_kv, 2)
    hn = rms_norm(x, g_kv_in) * (1 + scale) + shift
    lat = hn @ w_dkv
    ckv = rms_norm(lat[..., :KV_LORA], g_kv)
    kpe = apply_rope(lat[:, :, None, KV_LORA:], pos)[:, :, 0, :]
    return ckv, kpe

def mla_queries(h, pos, w_dq, g_q, w_uq):
    bsz, s, _ = h.shape
    q = (rms_norm(h @ w_dq, g_q) @ w_uq).reshape(bsz, s, MLA_HEADS, QK_NOPE + QK_ROPE)
    return q[..., :QK_NOPE], apply_rope(q[..., QK_NOPE:], pos)

def mla_attend_prompt(q_nope, q_pe, ckv, kpe, w_uk, w_uv):
    bsz, s, nh, _ = q_nope.shape
    nb = s // Q_BLOCK
    k_nope = jnp.einsum('bkc,chd->bkhd', ckv, w_uk)
    v = jnp.einsum('bkc,chd->bkhd', ckv, w_uv)
    k_pos = jnp.arange(s)

    def to_blocks(t):
        return jnp.moveaxis(t.reshape(bsz, nb, Q_BLOCK, nh, t.shape[-1]), 1, 0)

    def block(args):
        qn, qp, blk = args
        sc = jnp.einsum('bqhd,bkhd->bhqk', qn, k_nope) + jnp.einsum('bqhr,bkr->bhqk', qp, kpe)
        q_pos = blk * Q_BLOCK + jnp.arange(Q_BLOCK)
        sc = jnp.where(k_pos[None, :] <= q_pos[:, None], sc.astype(jnp.float32) * ATT_SCALE, -jnp.inf)
        p = jax.nn.softmax(sc, axis=-1).astype(v.dtype)
        return jnp.einsum('bhqk,bkhd->bqhd', p, v)

    o = lax.map(block, (to_blocks(q_nope), to_blocks(q_pe), jnp.arange(nb)))
    return jnp.moveaxis(o, 0, 1).reshape(bsz, s, nh * V_HEAD)

def mla_attend_sample(q_nope, q_pe, ckv_past, kpe_past, ckv_new, kpe_new, w_uk, w_uv):
    bsz, t, nh, _ = q_nope.shape
    n_past = ckv_past.shape[1]
    q_lat = jnp.einsum('bqhd,chd->bqhc', q_nope, w_uk)
    s_past = jnp.einsum('bqhc,bkc->bhqk', q_lat, ckv_past) + jnp.einsum('bqhr,bkr->bhqk', q_pe, kpe_past)
    s_new = jnp.einsum('bqhc,bkc->bhqk', q_lat, ckv_new) + jnp.einsum('bqhr,bkr->bhqk', q_pe, kpe_new)
    causal = jnp.tril(jnp.ones((t, t), bool))
    s_new = jnp.where(causal, s_new.astype(jnp.float32) * ATT_SCALE, -jnp.inf)
    sc = jnp.concatenate([s_past.astype(jnp.float32) * ATT_SCALE, s_new], axis=-1)
    p = jax.nn.softmax(sc, axis=-1).astype(ckv_new.dtype)
    o_lat = (jnp.einsum('bhqk,bkc->bqhc', p[..., :n_past], ckv_past)
             + jnp.einsum('bhqk,bkc->bqhc', p[..., n_past:], ckv_new))
    o = jnp.einsum('bqhc,chd->bqhd', o_lat, w_uv)
    return o.reshape(bsz, t, nh * V_HEAD)

def trunk(x, c, pos, conv_bufs, m_states, kv_past,
          g_norm1, g_norm2, w_ada, b_ada, w_up, w_conv, b_conv, w_down,
          w_m_in, b_m_gates, g_m_head, w_m_out,
          g_kv_in, w_ada_kv, b_ada_kv, w_dkv, g_kv, w_uk, w_uv,
          w_dq, g_q, w_uq, w_o, g_final):
    new_c, new_n, new_m, new_conv = [], [], [], []
    ckv = kpe = None
    for layer in range(DEPTH):
        sh1, sc1, gt1, sh2, sc2, gt2 = ada_mod(c, w_ada[layer], b_ada[layer], 6)
        if layer == N_A:
            ckv, kpe = shared_latent(x, c, pos, g_kv_in, w_ada_kv, b_ada_kv, w_dkv, g_kv)
        hn = rms_norm(x, g_norm1[layer]) * (1 + sc1) + sh1
        if layer < N_A:
            st = None if m_states is None else (m_states[0][layer], m_states[1][layer], m_states[2][layer])
            mix, (c_st, n_st, m_st) = mlstm_mixer(hn, w_m_in[layer], b_m_gates[layer],
                                                  g_m_head[layer], w_m_out[layer], st)
            new_c.append(c_st)
            new_n.append(n_st)
            new_m.append(m_st)
        else:
            j = layer - N_A
            q_nope, q_pe = mla_queries(hn, pos, w_dq[j], g_q[j], w_uq[j])
            if kv_past is None:
                att = mla_attend_prompt(q_nope, q_pe, ckv, kpe, w_uk, w_uv)
            else:
                att = mla_attend_sample(q_nope, q_pe, kv_past[0], kv_past[1], ckv, kpe, w_uk, w_uv)
            mix = att @ w_o[j]
        x = x + gt1 * mix
        hn = rms_norm(x, g_norm2[layer]) * (1 + sc2) + sh2
        f, buf = conv_ffn(hn, conv_bufs[layer], w_up[layer], w_conv[layer], b_conv[layer], w_down[layer])
        new_conv.append(buf)
        x = x + gt2 * f
    y = rms_norm(x, g_final)
    return y, jnp.stack(new_c), jnp.stack(new_n), jnp.stack(new_m), jnp.stack(new_conv), ckv, kpe

def setup_inputs(seed: int = 0) -> dict:
    key = jax.random.key(seed)
    ks = iter(jax.random.split(key, 48))

    def nrm(shape, scale=1.0):
        return scale * jax.random.normal(next(ks), shape, jnp.float32)

    D = D_MODEL
    n_pages = PAST_LEN // PAGE_SIZE
    n_used = DEC_BATCH * n_pages
    n_phys = n_used + n_used // 4
    x_prompt = nrm((BATCH, SEQ, D))
    x_sample = nrm((DEC_BATCH, DEC_SEQ, D))
    state_mlstm_C = nrm((N_A, DEC_BATCH, M_HEADS, M_DK, M_DV))
    state_mlstm_n = nrm((N_A, DEC_BATCH, M_HEADS, M_DK))
    state_mlstm_m = nrm((N_A, DEC_BATCH, M_HEADS))
    state_conv = nrm((DEPTH, DEC_BATCH, CONV_W - 1, D_FF))
    cache_ckv = nrm((n_phys, PAGE_SIZE, KV_LORA))
    cache_kpe = nrm((n_phys, PAGE_SIZE, QK_ROPE))
    page_table = jax.random.permutation(next(ks), n_phys)[:n_used].reshape(DEC_BATCH, n_pages).astype(jnp.int32)
    c_prompt = nrm((BATCH, D))
    c_sample = nrm((DEC_BATCH, D))
    g_norm1 = 1.0 + nrm((DEPTH, D), 0.05)
    g_norm2 = 1.0 + nrm((DEPTH, D), 0.05)
    w_ada = nrm((DEPTH, D, 6 * D), 0.5 * D ** -0.5)
    b_ada = nrm((DEPTH, 6 * D), 0.01)
    w_up = nrm((DEPTH, D, 2 * D_FF), D ** -0.5)
    w_conv = nrm((DEPTH, CONV_W, D_FF), CONV_W ** -0.5)
    b_conv = nrm((DEPTH, D_FF), 0.01)
    w_down = nrm((DEPTH, D_FF, D), D_FF ** -0.5)
    w_m_in = nrm((N_A, D, M_IN), D ** -0.5)
    b_m_gates = jnp.concatenate([nrm((N_A, M_HEADS), 0.1), 3.0 + nrm((N_A, M_HEADS), 0.1)], axis=-1)
    g_m_head = 1.0 + nrm((N_A, M_HEADS, M_DV), 0.05)
    w_m_out = nrm((N_A, M_HEADS * M_DV, D), (M_HEADS * M_DV) ** -0.5)
    g_kv_in = 1.0 + nrm((D,), 0.05)
    w_ada_kv = nrm((D, 2 * D), 0.5 * D ** -0.5)
    b_ada_kv = nrm((2 * D,), 0.01)
    w_dkv = nrm((D, KV_LORA + QK_ROPE), D ** -0.5)
    g_kv = 1.0 + nrm((KV_LORA,), 0.05)
    w_uk = nrm((KV_LORA, MLA_HEADS, QK_NOPE), KV_LORA ** -0.5)
    w_uv = nrm((KV_LORA, MLA_HEADS, V_HEAD), KV_LORA ** -0.5)
    w_dq = nrm((N_B, D, Q_LORA), D ** -0.5)
    g_q = 1.0 + nrm((N_B, Q_LORA), 0.05)
    w_uq = nrm((N_B, Q_LORA, MLA_HEADS * (QK_NOPE + QK_ROPE)), Q_LORA ** -0.5)
    w_o = nrm((N_B, MLA_HEADS * V_HEAD, D), (MLA_HEADS * V_HEAD) ** -0.5)
    g_final = 1.0 + nrm((D,), 0.05)
    return {'x_prompt': x_prompt, 'x_sample': x_sample,
            'state_mlstm_C': state_mlstm_C, 'state_mlstm_n': state_mlstm_n, 'state_mlstm_m': state_mlstm_m,
            'state_conv': state_conv, 'cache_ckv': cache_ckv, 'cache_kpe': cache_kpe,
            'page_table': page_table, 'c_prompt': c_prompt, 'c_sample': c_sample,
            'g_norm1': g_norm1, 'g_norm2': g_norm2, 'w_ada': w_ada, 'b_ada': b_ada,
            'w_up': w_up, 'w_conv': w_conv, 'b_conv': b_conv, 'w_down': w_down,
            'w_m_in': w_m_in, 'b_m_gates': b_m_gates, 'g_m_head': g_m_head, 'w_m_out': w_m_out,
            'g_kv_in': g_kv_in, 'w_ada_kv': w_ada_kv, 'b_ada_kv': b_ada_kv, 'w_dkv': w_dkv, 'g_kv': g_kv,
            'w_uk': w_uk, 'w_uv': w_uv, 'w_dq': w_dq, 'g_q': g_q, 'w_uq': w_uq, 'w_o': w_o,
            'g_final': g_final}

def reference(x_prompt, x_sample, state_mlstm_C, state_mlstm_n, state_mlstm_m, state_conv,
              cache_ckv, cache_kpe, page_table, c_prompt, c_sample,
              g_norm1, g_norm2, w_ada, b_ada, w_up, w_conv, b_conv, w_down,
              w_m_in, b_m_gates, g_m_head, w_m_out,
              g_kv_in, w_ada_kv, b_ada_kv, w_dkv, g_kv, w_uk, w_uv,
              w_dq, g_q, w_uq, w_o, g_final):
    weights = (g_norm1, g_norm2, w_ada, b_ada, w_up, w_conv, b_conv, w_down,
               w_m_in, b_m_gates, g_m_head, w_m_out,
               g_kv_in, w_ada_kv, b_ada_kv, w_dkv, g_kv, w_uk, w_uv,
               w_dq, g_q, w_uq, w_o, g_final)
    bp, s, _ = x_prompt.shape
    bs, t, _ = x_sample.shape
    past_len = page_table.shape[1] * cache_ckv.shape[1]

    conv0 = jnp.zeros((DEPTH, bp, CONV_W - 1, D_FF), x_prompt.dtype)
    y_p, c_p, n_p, m_p, conv_p, ckv_p, kpe_p = trunk(
        x_prompt, c_prompt, jnp.arange(s), conv0, None, None, *weights)

    ckv_past = cache_ckv[page_table].reshape(bs, past_len, KV_LORA)
    kpe_past = cache_kpe[page_table].reshape(bs, past_len, QK_ROPE)
    y_s, c_s, n_s, m_s, conv_s, ckv_s, kpe_s = trunk(
        x_sample, c_sample, past_len + jnp.arange(t), state_conv,
        (state_mlstm_C, state_mlstm_n, state_mlstm_m), (ckv_past, kpe_past), *weights)

    return (y_p, y_s, c_p, n_p, m_p, conv_p, ckv_p, kpe_p, c_s, n_s, m_s, conv_s, ckv_s, kpe_s)


_drawn_inputs = setup_inputs


def setup_inputs(seed=0):
    import zlib

    import numpy as np

    out = dict(_drawn_inputs(seed))
    spreads = {}
    factors = {'cache_ckv': 3.85,
     'cache_kpe': 7.117,
     'b_conv': 8.0,
     'g_m_head': 6.892,
     'b_ada_kv': 4.266,
     'g_q': 8.0}
    for name, (base, spread) in spreads.items():
        noise = np.random.default_rng([zlib.crc32(name.encode()), seed]).standard_normal(out[name].shape)
        drawn = base * np.exp(spread * noise) if base else spread * noise
        out[name] = __import__('jax').numpy.asarray(drawn.astype(out[name].dtype))
    for name, factor in factors.items():
        out[name] = (out[name] * factor).astype(out[name].dtype)
    return out
```

```python
from contextlib import ExitStack, contextmanager

import concourse.bass as bass
from concourse import mybir

F32 = mybir.dt.float32
F32R = mybir.dt.float32r
I32 = mybir.dt.int32
ALU = mybir.AluOpType
ACT = mybir.ActivationFunctionType
AX = mybir.AxisListType

P = 128
D = 1024
KT = D // P
SEQ = 1024
NS = 8
NT = SEQ + NS
CH = NT // 3
NC9 = NS + 1
HEADS = 4
DV = 256
NCK = SEQ // P
NF = 2816 // P
EPS = 1e-6
MH = 16
KVL = 256
QL = 384
ATT_SCALE = float(64 + 32) ** -0.5
BIG = 1e30

SH1, SC1, GT1, SH2, SC2, GT2 = 0, 8, 16, 24, 32, 40
MODL = 48
SHKV, SCKV = 96, 104
NMOD = 112
G_HEAD, GPH = 4, 3
G_FF = G_HEAD + GPH * HEADS

U_GATES = 0
U_HEAD, UPH = 1, 8
U_FF0 = U_HEAD + HEADS * UPH
FF_UNITS = 3 * NF
U_DKV = U_FF0 + FF_UNITS
U_DQ = U_DKV + 3
U_PAIR = U_DQ + 3
UPP = 6
U_FF1 = U_PAIR + 4 * UPP
NU = U_FF1 + FF_UNITS

T_N0 = 0
T_GATES = 1
T_COLS = 2
T_HEAD, TPH = 3, 22
T_N1 = T_HEAD + HEADS * TPH
T_FF0 = T_N1 + 1
TPF = 12
FF_FILLS = 4 + 10 * TPF + 8
T_N2 = T_FF0 + FF_FILLS
T_DKV = T_N2 + 1
T_DQ = T_DKV + 3
T_CKN = T_DQ + 3
T_QN = T_CKN + 1
T_PAIR, TPP, TP1 = T_QN + 1, 50, 21
TQ, TR, TK, TV = range(4)
T_SAMP = T_PAIR + 4 * TPP
TPS = 4
T_N3 = T_SAMP + NS * TPS
T_FF1 = T_N3 + 1
T_N4 = T_FF1 + FF_FILLS

N_SQ, N_HN = KT, KT + 1


PER = {"dve_m": 32, "act_n": 8, "dve_n": 74, "dve_z": 28}


class Steps:

    def __init__(self, eng, sem):
        self.eng, self.sem, self.base, self.k, self.i, self.per = eng, sem, 0, 0, None, 0

    def done(self, ins):
        ins.then_inc(self.sem, 1)
        self.k += 1

    def sync(self):
        at = self.base + self.k
        self.eng.wait_ge(self.sem, at if self.i is None else self.i * self.per + at)

    def link(self, ins):
        self.done(ins)
        self.sync()

    @contextmanager
    def loop(self, start, end, per):
        self.base += self.k - start * per
        self.k, self.per = 0, per
        with self.eng.Fori(start, end) as i:
            self.i = i
            yield i
            assert self.k == per, (self.k, per)
        self.base += end * per
        self.k, self.i = 0, None


def build(nc, t):
    with ExitStack() as ctx:
        program(nc, t, ctx)


def program(nc, t, ctx):
    def sb(name, shape, dt=F32, scope=ctx):
        return scope.enter_context(nc.sbuf_tensor(name, shape, dt))

    def sem(name):
        return ctx.enter_context(nc.semaphore(name))

    ps = ctx.enter_context(nc.psum_tensor("ps", [P, 8, 512], F32))
    psf = ps[:, :, :].rearrange("p b c -> p (b c)")

    def slot(T):
        s = 3 * (T % 2)
        return ps[:, s:s + 3, 0:CH]

    def flat(T, n, off=0):
        o = 1536 * (T % 2) + off
        return psf[:, o:o + n]

    START, LIMIT = 16512, 229344

    class Region:

        def __init__(self, at):
            self.at = at

        def __call__(self, name, shape, dt=F32):
            n = 4
            for d in shape[1:]:
                n *= d
            n = (n + 31) // 32 * 32
            out = nc.alloc_sbuf_tensor_at(name, shape, dt, offset=self.at)
            self.at += n
            assert self.at <= LIMIT, (name, self.at, LIMIT)
            return out

    R = Region(START)
    x = R("x", [P, KT, NT])
    raw = [R(f"w_raw{j}", [P, KT, P]) for j in range(2)]
    hi = [R(f"w_hi{j}", [P, KT, P], F32R) for j in range(2)]
    lo = [R(f"w_lo{j}", [P, KT, P], F32R) for j in range(2)]
    araw = [R(f"ada_raw{j}", [P, KT, P]) for j in range(2)]
    mod = R("mod", [P, NMOD, NC9])
    b_ada = R("b_ada", [P, NMOD])
    sc = R("silu_c", [P, KT, NC9])
    amul = R("norm_mul", [P, KT, NC9])
    gn = R("norm_gain", [P, 6, KT])
    gf = R("final_gain", [P, KT])
    ident = R("ident", [P, P])
    ones = R("ones", [P, P])
    nsm = R("norm_samples", [P, KT, NS])
    eps = R("eps", [P, 1])
    tmp = R("x_samples_add", [P, KT, NS])
    BASE = R.at

    R = Region(BASE)
    hnh_m, hnl_m = R("hn_head_m", [P, KT, NT], F32R), R("hn_rest_m", [P, KT, NT], F32R)
    o_nbuf = R.at
    nbuf_m = R("norm_buf_m", [P, 4160])
    o_pair = R.at
    dm, p_ = R("decay", [P, NCK, P]), R("p_m", [P, SEQ])
    wk, qw = R("wk", [P, NCK, P]), R("qw", [P, SEQ])
    R.at = o_pair
    oh, ol = R("o_head", [P, 2, NT], F32R), R("o_rest", [P, 2, NT], F32R)
    squares = Region(o_pair)("h_squares", [P, NCK, DV])
    o_hs = R.at
    hs = R("h_tokens", [P, NCK, DV + 1])
    va = R("v_aug", [P, NCK, DV + 1])
    o_bc = R.at
    bc = R("row_bcast", [P, 2, NT])
    cs = R("state_s", [P, NS, DV])
    caug = R("state_p", [P, DV + 1])
    ns_ = R("n_s", [P, NS])
    bs = R("emn_s", [P, NS])
    cols = R("cols", [P, HEADS, 3, NCK])
    colh = R("cols_head", [P, 3, NCK])
    cmask = R("chunk_mask", [P, P])
    kiw, prod = R("kiw", [P, NS]), R("prod", [P, NS])
    vs = R("v_rows", [NS, DV])
    sd, sh, sq2 = R("s_den", [P, 2, NS]), R("s_h", [P, 2, NS]), R("s_sq", [P, 2, NS])
    sv, hv, hd = R("s_var", [P, 2, NS]), R("h_var", [P, 3, NCK]), R("h_den", [P, 2, NCK])
    gh, ghl = R("g_head", [P, HEADS, 2]), R("g_head_now", [P, 2])
    bg, m0, mp = R("b_gates", [HEADS, 2]), R("m_old", [HEADS, NS]), R("m_prev", [HEADS, NCK])
    ada_rows = [R("ada_rows_m", [NC9, 2, 512])]
    acc_m = Region(o_hs)("norm_acc_m", [P, NT])
    rstd_m = Region(o_bc)("rstd_m", [P, NT])
    Q = Region(o_pair)
    g_, li, lf, m_ = (Q(n, [HEADS, NT]) for n in ("gate_g", "gate_li", "gate_lf", "gate_m"))
    Q = Region(o_hs)
    t3 = Q("gate_cols", [96, SEQ])
    rows = Q("gate_rows", [HEADS, 3, NT])
    Q = Region(o_bc + 4128)
    b_ = Q("gate_b", [HEADS, NT])
    Q = Region(o_bc + 8256)
    reset = Q("gate_reset", [HEADS, SEQ])
    nb = lambda t_, k, n=SEQ: t_[:, k * n:(k + 1) * n]
    M = dict(hnh=hnh_m, hnl=hnl_m, qT=nbuf_m[:, 0:NT], kT=nbuf_m[:, NT:2 * NT],
             vT=nbuf_m[:, 2 * NT:4 * NT].rearrange("p (j n) -> p j n", j=2),
             so=nbuf_m[:, 0:2 * NT].rearrange("p (j n) -> p j n", j=2),
             of=nbuf_m[:, 2 * NT:4 * NT].rearrange("p (j n) -> p j n", j=2),
             dm=dm, p=p_, wk=wk, qw=qw, oh=oh, ol=ol, hs=hs, va=va, bc=bc, cs=cs, caug=caug, ns=ns_,
             bs=bs, cols=cols, colh=colh, cmask=cmask, kiw=kiw, prod=prod, vs=vs, sd=sd, sh=sh,
             sq2=sq2, sv=sv, hv=hv, hd=hd, gh=gh, ghl=ghl, bg=bg, m0=m0, mp=mp, g=g_, li=li, lf=lf,
             m=m_, b=b_, t3=t3, rows=rows, reset=reset, tmp=tmp, squares=squares,
             act_per=22, dve_per=PER["dve_m"])
    B0 = dict(hnh=hnh_m, hnl=hnl_m, acc=acc_m, rstd=rstd_m,
              sq=nbuf_m[:, 0:2048].rearrange("p (j n) -> p j n", j=2),
              xr=nbuf_m[:, 0:2048].rearrange("p (j n) -> p j n", j=2),
              hf=nbuf_m[:, 2048:4096].rearrange("p (j n) -> p j n", j=2))

    R = Region(LIMIT - 2 * 4 * KT * P)
    hi.append(R("w_hi2", [P, KT, P], F32R))
    lo.append(R("w_lo2", [P, KT, P], F32R))
    TOP = LIMIT - 2 * 4 * KT * P
    ada_rows.append(Region(TOP - 4096)("ada_rows_f", [NC9, 2, 512]))

    def ffn_buffers(n):
        R = Region(BASE)
        d = {}
        d["hnh"], d["hnl"] = R(f"hn_head_f{n}", [P, KT, NT], F32R), R(f"hn_rest_f{n}", [P, KT, NT], F32R)
        nbuf = R(f"norm_buf_f{n}", [P, 4096])
        d["hh"], d["hl"] = R(f"h_head{n}", [P, 2, NT], F32R), R(f"h_rest{n}", [P, 2, NT], F32R)
        d["acc"] = R(f"norm_acc_f{n}", [P, NT])
        d["aext"] = R(f"a_ext{n}", [P, 2, 2 + NT])
        d["rstd"] = R(f"rstd_f{n}", [P, NT])
        d["htmp"] = R(f"h_tmp{n}", [P, 2, NT])
        d["cw"], d["cwl"] = R(f"conv_w{n}", [P, NF, 4]), R(f"conv_w_now{n}", [P, 2, 4])
        d["cb"], d["cbl"] = R(f"conv_buf{n}", [P, NF, 2, NS]), R(f"conv_buf_now{n}", [P, 2, 2, NS])
        d["co"], d["keep"] = R(f"conv_out{n}", [P, NF, 10]), R(f"conv_keep{n}", [P, 2, 10])
        d["cv"], d["sil"] = nbuf[:, 0:NT], nbuf[:, NT:2 * NT]
        d["sq"] = d["xr"] = nbuf[:, 0:2048].rearrange("p (j n) -> p j n", j=2)
        d["hf"] = nbuf[:, 2048:4096].rearrange("p (j n) -> p j n", j=2)
        d["tmp"] = tmp
        assert R.at <= TOP - 4096
        return d

    F0, F1 = ffn_buffers(0), ffn_buffers(1)

    R = Region(BASE)
    B1 = dict(F0, sq=R("norm_squares_f0", [P, 2, SEQ]), acc=R("norm_sum_f0", [P, NT]))

    R = Region(BASE)
    L = {}
    L["ckh"], L["ckl"] = R("ck_head", [P, 2, NT], F32R), R("ck_rest", [P, 2, NT], F32R)
    L["cos"], L["sin"] = R("cos", [P, NT]), R("sin", [P, NT])
    o_kpr = R.at
    L["kpr"] = R("k_rot", [P, NT])
    L["cks"], L["kps"] = R("ck_samples", [P, 2, NS]), R("k_rot_samples", [32, NS])
    qsn, qsp = R("q_samples", [64, MH, NS]), R("q_rot_samples", [32, MH, NS])
    o_L = R.at
    hn_L = [R("hn_head_l", [P, KT, NT], F32R)]
    hn_L.append(R("hn_rest_l", [P, KT, NT], F32R))
    nbuf_l = R("norm_buf_l", [P, 4 * NT])
    L["ckr"] = R("ck_raw", [P, 2, NT])
    L["sqt"] = nbuf_l[:, 3 * NT:4 * NT]
    acc_l = R("norm_acc_l", [P, NT])
    rstd_l = R("rstd_l", [P, NT])
    assert R.at <= TOP, (R.at, TOP)
    L["cqr"] = nbuf_l[:, 0:3 * NT].rearrange("p (j n) -> p j n", j=3)
    L["ck_sum"], L["cq_sum"] = acc_l[:, :], rstd_l[:, :]
    L["ta0"], L["tb0"] = L["sqt"], nbuf_l[:, 0:NT]
    BL = dict(hnh=hn_L[0], hnl=hn_L[1], acc=acc_l, rstd=rstd_l,
              sq=nbuf_l[:, 0:2048].rearrange("p (j n) -> p j n", j=2),
              xr=nbuf_l[:, 0:2048].rearrange("p (j n) -> p j n", j=2),
              hf=nbuf_l[:, 2048:4096].rearrange("p (j n) -> p j n", j=2))
    R = Region(o_L)
    sq_l = R("norm_squares_l", [P, 2, SEQ])
    B2 = dict(BL, sq=sq_l, acc=R("norm_sum_l", [P, NT]))
    R = Region(o_L)
    L["cqh"], L["cql"] = R("cq_head", [P, 3, NT], F32R), R("cq_rest", [P, 3, NT], F32R)
    N = dict(qsn=qsn, qsp=qsp, act_per=PER["act_n"], dve_per=PER["dve_n"])
    o_mask = R.at
    N["amask"] = R("causal_mask", [P, P])
    N["nm"], N["rs"], N["ri"] = R("neg_max", [P, 2]), R("row_sum", [P, 4]), R("row_inv", [P, 2])
    o_att = R.at
    N["q"], N["k"] = R("q_heads", [P, 2, SEQ]), R("k_heads", [P, 2, SEQ])
    N["v"] = R("v_tokens", [P, NCK, P])
    N["pex"] = R("p_exp", [P, 2, SEQ])
    N["pt"] = R("p_turned", [P, 4, 512])
    N["att"] = R("att_tokens", [P, NCK, P])
    N["ath"], N["atl"] = R("att_head", [P, 2, SEQ], F32R), R("att_rest", [P, 2, SEQ], F32R)
    N["ta"], N["tb"] = R("rot_a", [64, NT]), R("rot_b", [64, NT])
    R = Region(o_att)
    Z = {}
    Z["wuk"], Z["wuv"] = R("w_uk_turned", [64, MH, KVL]), R("w_uv_plain", [P, 2, SEQ])
    E = Region(BASE)
    sum_f1 = E("norm_sum_f1", [P, NT])
    early = [(E(f"pages_ckv{j}", [P, NCK, KVL]), E(f"pages_kpe{j}", [P, NCK, 32])) for j in range(2)]
    Z["pt"] = E("pages", [1, NS * NCK], I32)
    assert E.at <= o_kpr
    Z["kc"] = [early[j][0] for j in range(2)] + [R(f"pages_ckv{j}", [P, NCK, KVL]) for j in (2, 3)]
    Z["kp"] = [early[j][1] for j in range(2)] + [R(f"pages_kpe{j}", [P, NCK, 32]) for j in (2, 3)]
    Z["ckt"] = R("ck_rows", [NS, KVL])
    Q = Region(o_L)
    Z["cT"] = [R("keys_c0", [P, 2, SEQ + 1]), Q("keys_c1", [P, 2, SEQ + 1])]
    Z["kT"] = [R("keys_rot0", [32, SEQ + 1]), Q("keys_rot1", [32, SEQ + 1])]
    Z["pr"] = [R("probs0", [MH, SEQ + 1]), Q("probs1", [MH, SEQ + 1])]
    Z["ql"] = R("q_latent", [P, 2, NS, MH])
    Z["qb"], Z["qpb"] = R("q_latent_now", [P, 2, 2, MH]), R("q_rot_now", [32, 2, MH])
    Z["prT"], Z["prn"] = R("probs_turned", [P, 2, NCK, MH]), R("prob_new", [NS, 2, MH])
    Z["nm"], Z["rs"], Z["ri"] = R("z_neg_max", [MH, 2]), R("z_sum", [MH, 2]), R("z_inv", [MH, 2])
    Z["ol"], Z["olT"] = R("o_latent", [MH, 2, KVL]), R("o_latent_turned", [P, 2, MH, NS])
    Z["at"] = R("att_samples", [P, KT, NS])
    Z["dve_per"] = PER["dve_z"]
    B3 = dict(F1, sq=Q("norm_squares_f1", [P, 2, SEQ]), acc=sum_f1)
    assert R.at <= TOP and Q.at <= o_mask, (R.at, TOP)
    yb = Region(BASE)("y_tiles", [P, KT, NT])

    s_const = sem("s_const")
    x_loaded = sem("x_loaded")
    ones_ready = sem("ones_ready")
    silu_in = sem("silu_in")
    silu_ready = sem("silu_ready")
    scratch = sem("scratch")
    rows_ready = sem("rows_ready")
    row_dve = sem("row_dve")
    row_act = sem("row_act")
    head_loaded = sem("head_loaded")
    head_out = sem("head_out")
    head_free = sem("head_free")
    conv_loaded = sem("conv_loaded")
    w_split = sem("w_split")
    w_head = sem("w_head")
    a_used = sem("a_used")
    a_rows = sem("a_rows")
    a_turned = sem("a_turned")
    a_free = sem("a_free")
    act_step = sem("act_step")
    dve_step = sem("dve_step")
    full = sem("full")
    sq_ready = sem("sq_ready")
    sq_used = sem("sq_used")
    ss_ready = sem("ss_ready")
    xr_ready = sem("xr_ready")
    xr_used = sem("xr_used")
    hf_ready = sem("hf_ready")
    hn_ready = sem("hn_ready")
    x_done = sem("x_done")
    out_done = sem("out_done")
    y_ready = sem("y_ready")
    y_out = sem("y_out")
    h_ready = sem("h_ready")
    sil_ready = sem("sil_ready")
    cv_ready = sem("cv_ready")
    hh_ready = sem("hh_ready")
    co_ready = sem("co_ready")
    samp_pe = sem("samp_pe")
    samp_dve = sem("samp_dve")
    c_full = sem("c_full")
    c_upd = sem("c_upd")
    h_full = sem("h_full")
    h_free = sem("h_free")
    hs_ready = sem("hs_ready")
    hho_ready = sem("hho_ready")
    qw_ready = sem("qw_ready")
    dm_ready = sem("dm_ready")
    decay_ready = sem("decay_ready")
    cs_scaled = sem("cs_scaled")
    samp_var = sem("samp_var")
    samp_dev = sem("samp_dev")
    hsq_ready = sem("hsq_ready")
    hvar_ready = sem("hvar_ready")
    hdev_ready = sem("hdev_ready")
    of_ready = sem("of_ready")
    oh_ready = sem("oh_ready")
    aext_zero = sem("aext_zero")
    lat_ready = sem("lat_ready")
    lat_head = sem("lat_head")
    lat_split = sem("lat_split")
    latent_out = sem("latent_out")
    q_ready = sem("q_ready")
    nm_ready = sem("nm_ready")
    o_full = sem("o_full")
    o_free = sem("o_free")
    at_head = sem("at_head")
    samp_w = sem("samp_w")
    pages_in = sem("pages_in")
    kv_used = sem("kv_used")
    z_pe = sem("z_pe")
    z_dve = sem("z_dve")
    z_qb = sem("z_qb")
    z_pt = sem("z_pt")
    z_ptc = sem("z_ptc")
    z_ol = sem("z_ol")
    z_olc = sem("z_olc")
    z_ot = sem("z_ot")
    z_nm = sem("z_nm")
    tables_in = sem("tables_in")
    consts_dve = sem("consts_dve")
    w_loaded = [sem("w_loaded0"), sem("w_loaded1")]
    a_loaded = [sem("a_loaded0"), sem("a_loaded1")]
    free = [sem("free0"), sem("free1")]
    pt_full = [sem("pt_full0"), sem("pt_full1")]
    pt_copied = [sem("pt_copied0"), sem("pt_copied1")]
    kv_loaded = [sem(f"kv_loaded{j}") for j in range(4)]
    A = Steps(nc.scalar, act_step)

    def fl(eng, T, i=0, tper=0):
        eng.wait_ge(full, T + 1 + i * tper)

    def ev(eng, T, i=0, tper=0):
        eng.wait_ge(free[T % 2], T // 2 + 1 + i * (tper // 2))

    def take(T, i=0, tper=0):
        if not (isinstance(i, int) and T // 2 + i * (tper // 2) == 0):
            nc.tensor.wait_ge(free[T % 2], T // 2 + i * (tper // 2))

    def load_unit(u, i=0, per=0, n=KT):
        if not (isinstance(i, int) and u + i * per < 2):
            nc.sync.wait_ge(w_split, u - 1 + i * per)
        at = u + i * per
        nc.sync.dma_start(raw[u % 2][:, 0:n, :], t["w_units"][bass.ds(at, 1), :, 0:n, :]
                          .rearrange("a p k c -> p (a k) c")).then_inc(w_loaded[u % 2], 16)

    def split_unit(u, i, per, free_fill, tper, n=KT):
        pool, s = nc.gpsimd, ring(u + per)
        pool.wait_ge(w_loaded[u % 2], (u // 2 + 1) * 16 + i * (per // 2 * 16))
        if free_fill is not None:
            fl(pool, free_fill, i, tper)
        pool.tensor_tensor(hi[s][:, 0:n, :], raw[u % 2][:, 0:n, :],
                           ones[:, :].unsqueeze(1).to_broadcast([P, n, P]), ALU.mult).then_inc(w_head, 1)
        pool.wait_ge(w_head, u + 1 + i * per)
        pool.tensor_tensor(lo[s][:, 0:n, :], raw[u % 2][:, 0:n, :], hi[s][:, 0:n, :].bitcast(F32),
                           ALU.subtract).then_inc(w_split, 1)

    def ring(u):
        return (u % 2) if u < U_FF0 else (u - U_FF0) % 3

    def load_ada(u, i=0, per=0):
        if not (isinstance(i, int) and u + i * per < 2):
            nc.sync.wait_ge(a_used, u - 1 + i * per)
        at = u + i * per
        nc.sync.dma_start(araw[u % 2][:, :, :], t["ada_units"][bass.ds(at, 1)]
                          .rearrange("a p k c -> p (a k) c")).then_inc(a_loaded[u % 2], 16)

    def pe_ada_units(g, parts, bank, i=0, per=0, before=None):
        pe = nc.tensor
        if 0 in parts and before is not None:
            pe.wait_ge(a_free, before + i * per)
        for a in parts:
            pe.wait_ge(a_loaded[a % 2], (2 * g + a // 2 + 1) * 16 + i * (per * 32))
            for k in range(2):
                mm = pe.matmul(ps[0:NC9, bank, :], sc[:, 2 * a + k, :],
                               araw[a % 2][:, 4 * k:4 * k + 4, :].rearrange("p q c -> p (q c)"),
                               start=(a + k == 0), stop=(a + k == 4 and a == 3))
            mm.then_inc(a_used, 1)

    def dve_ada_rows(g, bank, i=0, per=0):
        nc.vector.wait_ge(a_used, 4 * g + 4 + i * (per * 4))
        nc.vector.tensor_copy(ada_rows[g >= G_FF - 1][:, bank - 6, :], ps[0:NC9, bank, :]).then_inc(a_rows, 1)

    def pe_ada_turn(g, bank, i=0, per=0):
        pe = nc.tensor
        pe.wait_ge(a_rows, g + 1 + i * per)
        for k in range(4):
            mm = pe.matmul(ps[:, bank, k * NC9:(k + 1) * NC9], ada_rows[g >= G_FF - 1][:, bank - 6, k * P:(k + 1) * P],
                           ident[0:NC9, 0:NC9], start=True, stop=True)
        mm.then_inc(a_turned, 1)

    def dve_ada(g, bank, i=0, per=0):
        dve = nc.vector
        dve.wait_ge(a_turned, g + 1 + i * per)
        at = 4 * g + i * (4 * per)
        dve.tensor_tensor(mod[:, bass.ds(at, 4), :],
                          ps[:, bank, 0:4 * NC9].rearrange("p (n c) -> p n c", c=NC9),
                          b_ada[:, bass.ds(at, 4)].unsqueeze(2).to_broadcast([P, 4, NC9]),
                          ALU.add).then_inc(a_free, 1)

    def products(out, wh, wl, xh, xl, cols, first, last):
        for p_, (w, v) in enumerate(((wh, xh), (wh, xl), (wl, xh))):
            for c, (a, b) in enumerate(cols):
                mm = nc.tensor.matmul(out(c), w, v[:, a:b], start=(first and p_ == 0),
                                      stop=(last and p_ == 2))
        return mm

    THIRDS = [(c * CH, (c + 1) * CH) for c in range(3)]

    def pe_up(u, i, per, T, tper, xh, xl, wait_k=None):
        pe, s = nc.tensor, ring(u + per)
        pe.wait_ge(w_split, u + 1 + i * per)
        take(T, i, tper)
        for kt in range(KT):
            if wait_k is not None:
                pe.wait_ge(hn_ready, wait_k + kt)
            mm = products(lambda c: slot(T)[:, c, :], hi[s][:, kt, :], lo[s][:, kt, :],
                          xh[:, kt, :], xl[:, kt, :], THIRDS, kt == 0, kt == KT - 1)
        mm.then_inc(full, 1)

    def pe_down(us, i, per, T, tper, tiles):
        nc.tensor.wait_ge(w_split, us[-1] + 1 + i * per)
        for m in range(KT):
            take(T + m, i, tper)
            for j, (u, (xh, xl)) in enumerate(zip(us, tiles)):
                mm = products(lambda c: slot(T + m)[:, c, :], hi[ring(u + per)][:, m, :],
                              lo[ring(u + per)][:, m, :], xh, xl, THIRDS, j == 0, j == len(us) - 1)
            mm.then_inc(full, 1)

    def dve_add_down(T, i, tper, gate, tmp):
        dve = nc.vector
        for m in range(KT):
            fl(dve, T + m, i, tper)
            g = mod[:, gate + m, 0:1]
            v = slot(T + m)
            dve.scalar_tensor_tensor(x[:, m, 0:2 * CH].rearrange("p (c n) -> p c n", n=CH),
                                     v[:, 0:2, :], g,
                                     x[:, m, 0:2 * CH].rearrange("p (c n) -> p c n", n=CH),
                                     ALU.mult, ALU.add)
            dve.scalar_tensor_tensor(x[:, m, 2 * CH:SEQ], v[:, 2, 0:SEQ - 2 * CH], g,
                                     x[:, m, 2 * CH:SEQ], ALU.mult, ALU.add).then_inc(x_done, 1)
            dve.tensor_tensor(tmp[:, m, :], v[:, 2, SEQ - 2 * CH:CH], mod[:, gate + m, 1:NC9],
                              ALU.mult).then_inc(free[(T + m) % 2], 1)
        ev(dve, T + KT - 1, i, tper)
        dve.tensor_tensor(x[:, :, SEQ:NT], x[:, :, SEQ:NT], tmp[:, :, :], ALU.add)\
           .then_inc(x_done, 1)

    def act_squares(n, x_final, B):
        act = nc.scalar
        for k in range(KT):
            x_final(k)
            used = 6 * n + (0 if k < 2 else max(1, k - 2))
            if used:
                act.wait_ge(sq_used, used)
            act.activation(B["sq"][:, k % 2, :], x[:, k, 0:SEQ], ACT.Square).then_inc(sq_ready, 1)
        x_final(KT)
        act.activation(nsm[:, :, :], x[:, :, SEQ:NT], ACT.Square).then_inc(sq_ready, 1)

    def x_in(k):
        nc.scalar.wait_ge(x_loaded, 16 * KT)

    def x_added(xd):
        return lambda k: nc.scalar.wait_ge(x_done, xd + k + 1)

    def pool_sum_squares(n, B):
        pool, acc, sq = nc.gpsimd, B["acc"], B["sq"]
        for k in range(1, KT - 1):
            pool.wait_ge(sq_ready, 9 * n + k + 1)
            if k > 1:
                pool.wait_ge(sq_used, 6 * n + k - 1)
            pool.tensor_tensor(acc[:, 0:SEQ], sq[:, 0, :] if k == 1 else acc[:, 0:SEQ], sq[:, k % 2, :],
                               ALU.add).then_inc(sq_used, 1)

    def dve_sum_samples(n, B):
        nc.vector.wait_ge(sq_ready, 9 * n + 9)
        nc.vector.tensor_reduce(B["acc"][:, SEQ:NT], nsm[:, :, :].rearrange("p k s -> p s k"),
                                AX.X, ALU.add).then_inc(ss_ready, 1)

    SUMS = [(0, 512), (512, SEQ), (SEQ, NT)]

    def pe_total(n, r, T, B):
        pe = nc.tensor
        pe.wait_ge(sq_used, 6 * n + 6)
        take(T)
        for a, b in SUMS[:2]:
            pe.matmul(flat(T, b - a, a), ones[:, :], B["acc"][:, a:b], start=True, stop=False)
        pe.wait_ge(sq_ready, 9 * n + 8)
        for a, b in SUMS[:2]:
            pe.matmul(flat(T, b - a, a), ones[:, :], B["sq"][:, 1, a:b], start=False, stop=True)
        pe.wait_ge(ss_ready, r + 1)
        pe.matmul(flat(T, NS, SEQ), ones[:, :], B["acc"][:, SEQ:NT], start=True, stop=True)\
          .then_inc(full, 1)

    def act_std(T, width, dst):
        act = nc.scalar
        fl(act, T)
        act.activation(dst, flat(T, NT), ACT.Sqrt, scale=1.0 / width, bias=eps[:, 0:1])\
           .then_inc(free[T % 2], 1)

    def dve_norm_out(n, T, gain, scale_tile, shift_tile, B, S, used=None, keep=False):
        dve = nc.vector
        hnh, hnl, xr, hf, rstd = B["hnh"], B["hnl"], B["xr"], B["hf"], B["rstd"]
        S.done(dve.scalar_tensor_tensor(amul[:, :, :], mod[:, scale_tile:scale_tile + KT, :], 1.0,
                                        gn[:, gain, :].unsqueeze(2).to_broadcast([P, KT, NC9]),
                                        ALU.add, ALU.mult))
        if not keep:
            ev(dve, T)
            S.link(dve.reciprocal(rstd[:, :], rstd[:, :]))
        for k in range(KT + 1):
            if k < KT:
                if k >= 2 or n:
                    dve.wait_ge(xr_used, 8 * n + max(0, k - 1))
                dve.tensor_tensor(xr[:, k % 2, :], x[:, k, 0:SEQ], rstd[:, 0:SEQ], ALU.mult)\
                   .then_inc(xr_ready, 1)
            if k == 1:
                S.link(dve.tensor_tensor(nsm[:, :, :], x[:, :, SEQ:NT],
                                         rstd[:, SEQ:NT].unsqueeze(1).to_broadcast([P, KT, NS]), ALU.mult))
                S.link(dve.tensor_tensor(nsm[:, :, :], nsm[:, :, :], amul[:, :, 1:NC9], ALU.mult))
                S.link(dve.tensor_tensor(nsm[:, :, :], nsm[:, :, :],
                                         mod[:, shift_tile:shift_tile + KT, 1:NC9], ALU.add))
                if used is not None:
                    fl(dve, used)
                S.link(dve.tensor_copy(hnh[:, :, SEQ:NT], nsm[:, :, :]))
                dve.tensor_tensor(hnl[:, :, SEQ:NT], nsm[:, :, :], hnh[:, :, SEQ:NT].bitcast(F32),
                                  ALU.subtract).then_inc(hn_ready, 1)
            if k:
                dve.wait_ge(hf_ready, 8 * n + k)
                dve.tensor_tensor(hnl[:, k - 1, 0:SEQ], hf[:, (k - 1) % 2, :],
                                  hnh[:, k - 1, 0:SEQ].bitcast(F32), ALU.subtract)\
                   .then_inc(hn_ready, 1)

    def act_norm_out(n, shift_tile, B, used=None):
        act = nc.scalar
        if used is not None:
            fl(act, used)
        for k in range(KT):
            act.wait_ge(xr_ready, 8 * n + k + 1)
            if k >= 2:
                act.wait_ge(hn_ready, 9 * n + k)
            act.activation(B["hf"][:, k % 2, :], B["xr"][:, k % 2, :], ACT.Identity,
                           bias=mod[:, shift_tile + k, 0:1], scale=amul[:, k, 0:1])\
               .then_inc(xr_used, 1)
            act.wait_ge(xr_used, 8 * n + k + 1)
            act.activation(B["hnh"][:, k, 0:SEQ], B["hf"][:, k % 2, :], ACT.Copy).then_inc(hf_ready, 1)

    def ff_units():
        fills = [0, 1, 2, 3] + [4, 5, 13, 13, 14, 15]
        return fills

    def sp_ffn(U, ada, l, F):
        def adas(u, i=0):
            if ada is not None:
                for k in range(4):
                    load_ada(u + k, i, 4)

        for k in range(2):
            load_unit(U + k)
        fl(nc.sync, (T_N1, T_N3)[l])
        nc.sync.dma_start(F["cw"][:, :, :], t["conv_w"][l]).then_inc(conv_loaded, 16)
        nc.sync.dma_start(F["cb"][:, :, :, :], t["state_conv"][l]).then_inc(conv_loaded, 16)
        for k in range(2, 4):
            load_unit(U + k)
        if ada is not None:
            for g in range(2):
                adas(4 * (ada + g))
        with nc.sync.Fori(1, 11) as i:
            for k in range(6):
                load_unit(U + 4 - 6 + k, i, 6)
            adas(4 * (ada + 2 - 1) if ada is not None else 0, i)
        for k in range(2):
            load_unit(U + 64 + k)

    def pool_ffn(U, T, last):
        fills = ff_units()
        for k in range(4):
            split_unit(U + k, 0, 0, last if k < 3 else T, 0)
        with nc.gpsimd.Fori(1, 11) as i:
            for k in range(6):
                split_unit(U + 4 + k - 6, i, 6, T + fills[4 + k - 3] - 12, 12)
        for k in range(2):
            split_unit(U + 64 + k, 0, 0, T + 9 * 12 + fills[4 + k + 3], 0)

    def pe_ffn(n, U, T, F, ada):
        pe = nc.tensor
        hnh, hnl, hh, hl = F["hnh"], F["hnl"], F["hh"], F["hl"]
        for f in range(2):
            for g in range(2):
                pe_up(U + 2 * f + g, 0, 0, T + 2 * f + g, 0, hnh, hnl,
                      9 * n + 2 if f + g == 0 else None)
        if ada is not None:
            for g in range(2):
                pe_ada_units(ada + g, range(4), 6 + g, before=ada if g == 0 else None)
            for g in range(2):
                pe_ada_turn(ada + g, 6 + g)
        base = 22 * (1 if n > 2 else 0)

        def down(i, per, tper, U2, T2):
            pe.wait_ge(h_ready, base + 2 * i)
            pe_down([U2, U2 + 1], i, per, T2, tper, [(hh[:, f, :], hl[:, f, :]) for f in range(2)])

        with pe.Fori(1, 11) as i:
            for g in range(2):
                pe_up(U + 4 + g - 6, i, 6, T + 4 + g - 12, 12, hnh, hnl)
            if ada is not None:
                pe_ada_units(ada + 2 - 1, range(4), 6, i, 1, ada + 2 - 1)
            down(i, 6, 12, U + 6 - 6, T + 6 - 12)
            if ada is not None:
                pe_ada_turn(ada + 2 - 1, 6, i, 1)
            for g in range(2):
                pe_up(U + 8 + g - 6, i, 6, T + 14 + g - 12, 12, hnh, hnl)
        down(11, 0, 0, U + 64, T + 4 + 120)

    def conv_tile(S_dve, F, f, i, T, tper, hbase):
        dve = nc.vector
        ae, cv, si, ht, hh, hl = F["aext"], F["cv"], F["sil"], F["htmp"], F["hh"], F["hl"]
        w = lambda j: F["cwl"][:, f, j:j + 1]
        a = ae[:, f, :]
        ev(dve, T, i, tper)
        if not (isinstance(i, int) and hbase + 2 * i + f == 0):
            dve.wait_ge(sil_ready, hbase + 2 * i + f)
        S_dve.done(dve.tensor_scalar(cv[:, 0:SEQ], a[:, 2:2 + SEQ], w(2), w(3), ALU.mult, ALU.add))
        S_dve.done(dve.tensor_scalar(cv[:, SEQ:NT], a[:, 2 + SEQ:], w(2), w(3), ALU.mult, ALU.add))
        S_dve.done(dve.tensor_copy(F["keep"][:, f, 0:2], a[:, SEQ:SEQ + 2]))
        S_dve.link(dve.tensor_copy(F["keep"][:, f, 2:10], a[:, 2 + SEQ:]))
        S_dve.done(dve.scalar_tensor_tensor(cv[:, 0:SEQ], a[:, 1:1 + SEQ], w(1), cv[:, 0:SEQ],
                                            ALU.mult, ALU.add))
        S_dve.link(dve.scalar_tensor_tensor(cv[:, SEQ:NT], F["cbl"][:, f, 1, :], w(1), cv[:, SEQ:NT],
                                            ALU.mult, ALU.add))
        S_dve.done(dve.scalar_tensor_tensor(cv[:, 0:SEQ], a[:, 0:SEQ], w(0), cv[:, 0:SEQ],
                                            ALU.mult, ALU.add))
        dve.scalar_tensor_tensor(cv[:, SEQ:NT], F["cbl"][:, f, 0, :], w(0), cv[:, SEQ:NT],
                                 ALU.mult, ALU.add).then_inc(cv_ready, 1)
        fl(dve, T + 1, i, tper)
        dve.wait_ge(sil_ready, hbase + 2 * i + f + 1)
        dve.tensor_tensor(ht[:, f, :].rearrange("p (c n) -> p c n", n=CH),
                          si[:, :].rearrange("p (c n) -> p c n", n=CH), slot(T + 1),
                          ALU.mult).then_inc(free[(T + 1) % 2], 1)

    def rest_of_h(F, f, i, hbase):
        nc.vector.wait_ge(hh_ready, hbase + 2 * i + f + 1)
        nc.vector.tensor_tensor(F["hl"][:, f, :], F["htmp"][:, f, :], F["hh"][:, f, :].bitcast(F32),
                                ALU.subtract).then_inc(h_ready, 1)

    def dve_ffn(S, n, layer, T, F, gate, ada):
        dve = nc.vector
        hbase = 22 * layer
        dve.wait_ge(conv_loaded, 32 * (layer + 1))
        dve.memset(F["aext"][:, :, 0:2], 0.0).then_inc(aext_zero, 1)

        def round_(i, tper, T2, first):
            S.done(dve.tensor_copy(F["cwl"][:, :, :], F["cw"][:, bass.ds(2 * i, 2), :]))
            S.link(dve.tensor_copy(F["cbl"][:, :, :, :], F["cb"][:, bass.ds(2 * i, 2), :, :]))
            conv_tile(S, F, 0, i, T2, tper, hbase)
            if ada is not None and first:
                for g in range(2):
                    dve_ada_rows(ada + g, 6 + g)
            elif ada is not None:
                dve_ada_rows(ada + 2 - 1, 6, i, 1)
            if not first:
                dve_add_down(T2 + 2, i, tper, gate, F["tmp"])
            if ada is not None and first:
                for g in range(2):
                    dve_ada(ada + g, 6 + g)
            elif ada is not None:
                dve_ada(ada + 2 - 1, 6, i, 1)
            rest_of_h(F, 0, i, hbase)
            conv_tile(S, F, 1, i, T2 + (2 if first else 10), tper, hbase)
            S.done(dve.tensor_copy(F["co"][:, bass.ds(2 * i, 2), :], F["keep"][:, :, :]))
            rest_of_h(F, 1, i, hbase)

        round_(0, 0, T, True)
        per = 2 + 14 + 1
        with S.loop(1, 11, per) as i:
            round_(i, 12, T + 4 - 12, False)
        dve_add_down(T + 124, 0, 0, gate, F["tmp"])
        S.sync()
        dve.sem_inc(co_ready, 1)

    def act_ffn(n, layer, T, F):
        act = nc.scalar
        hbase = 22 * layer

        def tile(f, i, T2, tper, first):
            if not first:
                act.wait_ge(cv_ready, hbase + 2 * i + f - 1)
            elif layer:
                act.wait_ge(cv_ready, hbase)
            if f == 0 and first:
                act.wait_ge(aext_zero, layer + 1)
            fl(act, T2, i, tper)
            act.activation(F["aext"][:, f, 2:].rearrange("p (c n) -> p c n", n=CH), slot(T2), ACT.Copy)\
               .then_inc(free[T2 % 2], 1)
            act.wait_ge(cv_ready, hbase + 2 * i + f + 1)
            act.activation(F["sil"][:, :], F["cv"][:, :], ACT.Silu).then_inc(sil_ready, 1)
            ev(act, T2 + 1, i, tper)
            if not first:
                fl(act, T + 13 - 12, i, 12)
            act.activation(F["hh"][:, f, :], F["htmp"][:, f, :], ACT.Copy).then_inc(hh_ready, 1)

        for f in range(2):
            tile(f, 0, T + 2 * f, 0, True)
        with act.Fori(1, 11) as i:
            for f in range(2):
                tile(f, i, T + 4 + 10 * f - 12, 12, False)

    def sp_mlstm(M):
        sp = nc.sync
        rows, bc, bs = M["rows"], M["bc"], M["bs"]
        sp.wait_ge(rows_ready, 1)
        sp.dma_start(t["row_scratch"], rows[:, :, :]).then_inc(scratch, 16)
        sp.dma_start(t["m_prompt"], M["m"][:, SEQ - 1:SEQ]).then_inc(out_done, 16)
        sp.dma_start(t["m_sample"], M["m"][:, SEQ:NT]).then_inc(out_done, 16)
        sp.wait_ge(scratch, 16)
        sp.wait_ge(out_done, 32)

        def head_loads(h):
            rs = t["row_scratch"][bass.ds(h, 1)]
            sp.dma_start(bc[:, :, :], rs[:, 0:2, :].to_broadcast([P, 2, NT])).then_inc(head_loaded, 16)
            sp.dma_start(bs[:, :], rs[:, 2, SEQ:NT].to_broadcast([P, NS])).then_inc(head_loaded, 16)
            sp.dma_start(M["cs"][:, :, :], t["state_C"][bass.ds(h, 1)].rearrange("h b d v -> d (h b) v"))\
              .then_inc(head_loaded, 16)
            sp.dma_start(M["ns"][:, :], t["state_n"][bass.ds(h, 1)].rearrange("h d b -> d (h b)"))\
              .then_inc(head_loaded, 16)

        def head_outs(h):
            sp.dma_start(t["C_prompt"][bass.ds(h, 1)].rearrange("h d v -> d (h v)"), M["caug"][:, 0:DV])\
              .then_inc(head_out, 16)
            sp.dma_start(t["n_prompt"][bass.ds(h, 1)].rearrange("h d v -> d (h v)"), M["caug"][:, DV:DV + 1])\
              .then_inc(head_out, 16)
            sp.dma_start(t["C_sample"][bass.ds(h, 1)].rearrange("h b d v -> d (h b) v"), M["cs"][:, :, :])\
              .then_inc(head_out, 16)
            sp.dma_start(t["n_sample"][bass.ds(h, 1)].rearrange("h d b -> d (h b)"), M["ns"][:, :])\
              .then_inc(head_out, 16)

        def units(h, ks):
            for k in ks:
                load_unit(U_HEAD + k, h, UPH)

        def ada(h, ks):
            for k in ks:
                load_ada(4 * G_HEAD + k, h, 4 * GPH)

        def rest_of_head(h):
            units(h, range(2, 4))
            ada(h, range(2))
            units(h, range(4, 6))
            ada(h, range(2, 4 * GPH))
            units(h, range(6, 8))

        head_loads(0)
        units(0, range(2))
        rest_of_head(0)
        with sp.Fori(1, HEADS) as h:
            units(h, range(2))
            sp.wait_ge(head_free, h)
            head_outs(h - 1)
            sp.wait_ge(head_out, 64 * h)
            head_loads(h)
            rest_of_head(h)
        sp.wait_ge(head_free, HEADS)
        head_outs(HEADS - 1)
        sp.wait_ge(head_out, 64 * HEADS)

    def pool_mlstm():
        split_unit(0, 0, 0, None, 0)
        fills = [0, 1, 2, 3, 10, 11, 21, 21]
        with nc.gpsimd.Fori(0, HEADS) as h:
            for k in range(UPH):
                if k == 0:
                    f = T_HEAD - 1
                elif k == 1:
                    f = T_HEAD - 1
                else:
                    f = T_HEAD + fills[k - 2]
                split_unit(U_HEAD + k, h, UPH, f, TPH)

    def gate_rows(S, M):
        dve = nc.vector
        g, li, lf, m, b, rows, t3 = M["g"], M["li"], M["lf"], M["m"], M["b"], M["rows"], M["t3"]
        S.done(dve.memset(t3[:, :], 0.0))
        fl(dve, T_GATES)
        v = slot(T_GATES)
        c3 = lambda a: a.rearrange("p (c n) -> p c n", n=CH)
        S.done(dve.tensor_scalar(c3(li[:, :]), v[0:HEADS], M["bg"][:, 0:1], None, ALU.add))
        dve.tensor_copy(c3(g[:, :]), v[64:64 + HEADS]).then_inc(free[T_GATES % 2], 1)
        ev(dve, T_GATES)
        S.link(dve.tensor_scalar(g[:, :], g[:, :], M["bg"][:, 1:2], None, ALU.add))
        S.link(dve.tensor_scalar(lf[:, :], g[:, :], 0.0, None, ALU.min))
        S.done(dve.scalar_tensor_tensor(m[:, :], g[:, :], -1.0, g[:, :], ALU.mult, ALU.max))
        S.sync()
        dve.sem_inc(row_dve, 1)
        dve.wait_ge(row_act, 1)
        S.link(dve.tensor_tensor(lf[:, :], lf[:, :], g[:, :], ALU.subtract))
        S.done(dve.tensor_tensor_scan(m[:, 0:SEQ], lf[:, 0:SEQ], li[:, 0:SEQ], 0.0, ALU.add, ALU.max))
        S.done(dve.tensor_tensor_scan(b[:, 0:SEQ], M["reset"][:, :], lf[:, 0:SEQ], 0.0, ALU.mult, ALU.add))
        S.link(dve.tensor_tensor(b[:, SEQ:NT], lf[:, SEQ:NT], M["m0"][:, :], ALU.add))
        S.link(dve.tensor_tensor(m[:, SEQ:NT], b[:, SEQ:NT], li[:, SEQ:NT], ALU.max))
        S.link(dve.tensor_tensor(rows[:, 0, :], b[:, :], m[:, :], ALU.subtract))
        S.done(dve.tensor_tensor(t3[0:HEADS, :], li[:, 0:SEQ], b[:, 0:SEQ], ALU.subtract))
        S.done(dve.memset(M["mp"][:, 0:1], 0.0))
        ck = lambda a: a.rearrange("p (c n) -> p c n", n=P)
        S.done(dve.tensor_copy(M["mp"][:, 1:NCK], ck(m[:, 0:SEQ])[:, 0:NCK - 1, P - 1]))
        S.link(dve.tensor_copy(rows[:, 1, SEQ:NT], rows[:, 0, SEQ:NT]))
        S.done(dve.tensor_tensor(ck(rows[:, 1, 0:SEQ]), ck(rows[:, 0, 0:SEQ]),
                                 M["mp"][:, :].unsqueeze(2).to_broadcast([HEADS, NCK, P]), ALU.add))
        S.done(dve.tensor_tensor(rows[:, 0, SEQ:NT], li[:, SEQ:NT], m[:, SEQ:NT], ALU.subtract))
        S.done(dve.tensor_tensor(ck(g[:, 0:SEQ]), ck(t3[0:HEADS, :]),
                                 ck(rows[:, 0, 0:SEQ])[:, :, P - 1:P].to_broadcast([HEADS, NCK, P]),
                                 ALU.add))
        S.sync()
        dve.sem_inc(row_dve, 1)
        fl(dve, T_COLS)
        dve.tensor_copy(M["cols"][:, :, :, :].rearrange("p h q c -> p c q h"),
                        flat(T_COLS, SEQ).rearrange("p (c q z) -> p c q z", c=NCK, z=32)[:, :, 0:3, 0:HEADS])\
           .then_inc(free[T_COLS % 2], 1)

    def act_rows(M):
        act = nc.scalar
        g, m, rows, t3 = M["g"], M["m"], M["rows"], M["t3"]
        act.wait_ge(row_dve, 1)
        A.link(act.activation(g[:, :], m[:, :], ACT.Exp, scale=-1.0))
        act.activation(g[:, :], g[:, :], ACT.Ln, bias=1.0).then_inc(row_act, 1)
        act.wait_ge(row_dve, 2)
        A.done(act.activation(rows[:, 1, :], rows[:, 1, :], ACT.Exp))
        A.done(act.activation(rows[:, 0, SEQ:NT], rows[:, 0, SEQ:NT], ACT.Exp))
        A.done(act.activation(rows[:, 2, :], m[:, :], ACT.Exp, scale=-1.0))
        A.done(act.activation(t3[32:32 + HEADS, :], g[:, 0:SEQ], ACT.Exp))
        A.done(act.activation(t3[64:64 + HEADS, :], m[:, 0:SEQ], ACT.Exp, scale=-1.0))
        A.sync()
        act.sem_inc(rows_ready, 1)

    def pe_mlstm(M):
        pe = nc.tensor
        hnh, hnl = M["hnh"], M["hnl"]
        pe_up(0, 0, 0, T_GATES, 0, hnh, hnl, 2)
        pe.wait_ge(rows_ready, 1)
        take(T_COLS)
        for c in range(NCK):
            mm = pe.transpose(flat(T_COLS, 96, c * P), M["t3"][:, c * P:(c + 1) * P], ident[0:96, 0:96])
        mm.then_inc(full, 1)
        qT, kT, vT, va, p_, wk, qw, ca, hs = (M[n] for n in ("qT", "kT", "vT", "va", "p", "wk", "qw", "caug", "hs"))
        ck = lambda a, c: a[:, c * P:(c + 1) * P]
        with pe.Fori(0, HEADS) as h:
            T = lambda k: T_HEAD + k
            for k in range(4):
                pe_up(U_HEAD + k, h, UPH, T(k), TPH, hnh, hnl)
            pe_ada_units(G_HEAD, range(2), 6, h, GPH, G_HEAD)
            for k, src in ((4, kT[:, :]), (5, vT[:, 0, :]), (6, vT[:, 1, :])):
                ev(pe, T(k - 3), h, TPH)
                take(T(k), h, TPH)
                for c in range(NCK):
                    mm = pe.transpose(flat(T(k), P, c * P), ck(src, c), ident[:, :])
                mm.then_inc(full, 1)
            ev(pe, T(0), h, TPH)
            take(T(7), h, TPH)
            for c in range(NCK):
                mm = pe.matmul(flat(T(7), P, c * P), ck(kT, c), ck(qT, c), start=True, stop=True)
            mm.then_inc(full, 1)
            take(T(8), h, TPH)
            for j in range(2):
                mm = pe.transpose(flat(T(8), P, 1024 + j * P)[0:NS], vT[:, j, SEQ:NT], ident[:, :])
            mm.then_inc(samp_pe, 1)
            pe_ada_units(G_HEAD, range(2, 4), 6, h, GPH)
            for g in range(2):
                pe.wait_ge(samp_dve, 1 + g + 5 * h)
                for b in range(4):
                    bb = 4 * g + b
                    mm = pe.matmul(flat(T(8), DV, b * DV), ident[0:NS, bb:bb + 1].to_broadcast([NS, P]),
                                   M["vs"][:, :], start=True, stop=True)
                mm.then_inc(samp_pe, 1)
            pe.wait_ge(samp_dve, 4 + 5 * h)
            pe.matmul(flat(T(8), NS, 1024), ones[:, :], M["prod"][:, :], start=True, stop=True)
            for j in range(2):
                for b in range(NS):
                    o = 1024 + NS + j * NS + b
                    mm = pe.matmul(flat(T(8), 1, o), M["cs"][:, b, j * P:(j + 1) * P],
                                   qT[:, SEQ + b:SEQ + b + 1], start=True, stop=True)
            mm.then_inc(samp_pe, 1)
            pe.wait_ge(samp_dve, 5 + 5 * h)
            for j in range(2):
                mm = pe.matmul(flat(T(8), NS, 1024 + 64), ones[:, :], M["sq2"][:, j, :],
                               start=(j == 0), stop=(j == 1))
            mm.then_inc(full, 1)
            for k in (4, 5, 6, 7):
                ev(pe, T(k), h, TPH)
            pe.wait_ge(qw_ready, 1 + h)
            pe_ada_turn(G_HEAD, 6, h, GPH)
            take(T(9), h, TPH)
            for c in range(NCK):
                if c == 4:
                    pe_ada_turn(G_HEAD + 1, 7, h, GPH)
                pe_ada_units(G_HEAD + 1 + c // 4, [c % 4], 7 - c // 4, h, GPH,
                             G_HEAD + c // 4)
                if c >= 2:
                    pe.wait_ge(h_free, c - 1 + 8 * h)
                H = flat(T(9), DV + 1, 512 * (c % 2))
                pe.matmul(H, ck(p_, c), va[:, c, :], start=True, stop=False)
                pe.wait_ge(c_upd, 1 + c + 8 * h)
                pe.matmul(flat(T(9), DV + 1, 1024), wk[:, c, :], va[:, c, :], start=True, stop=True)\
                  .then_inc(c_full, 1)
                mm = pe.matmul(H, ck(qw, c), ca[:, :], start=False, stop=True)
                mm.then_inc(full if c == NCK - 1 else h_full, 1)
            for k in (4, 5):
                pe_up(U_HEAD + k, h, UPH, T(k + 6), TPH, hnh, hnl)
                if k == 4:
                    pe_ada_turn(G_HEAD + 2, 6, h, GPH)
            for j in range(2):
                take(T(12 + j), h, TPH)
                if j == 0:
                    pe.wait_ge(hs_ready, 2 + 2 * h)
                for c in range(NCK):
                    mm = pe.transpose(flat(T(12 + j), P, c * P), hs[:, c, j * P:(j + 1) * P], ident[:, :])
                mm.then_inc(full, 1)
            pe.wait_ge(hho_ready, 2 + 2 * h)
            pe_down([U_HEAD + 6, U_HEAD + 7], h, UPH, T(14), TPH,
                    [(M["oh"][:, j, :], M["ol"][:, j, :]) for j in range(2)])

    def act_mlstm(M):
        act = nc.scalar
        act_rows(M)
        with A.loop(0, HEADS, M["act_per"]) as h:
            T = lambda k: T_HEAD + k
            c3 = lambda a: a.rearrange("p (c n) -> p c n", n=CH)

            def evac(k, dst, func=ACT.Copy, **kw):
                fl(act, T(k), h, TPH)
                act.activation(c3(dst), slot(T(k)), func, **kw).then_inc(free[T(k) % 2], 1)

            evac(0, M["qT"][:, :], scale=float(P) ** -0.5)
            evac(1, M["kT"][:, :])
            evac(2, M["vT"][:, 0, :])
            evac(3, M["vT"][:, 1, :])
            act.wait_ge(dm_ready, 1 + h)
            act.activation(M["dm"][:, :, :], M["dm"][:, :, :], ACT.Exp).then_inc(decay_ready, 1)
            fl(act, T(4), h, TPH)
            for c in range(NCK):
                ins = act.activation(M["wk"][:, c, :], flat(T(4), P, c * P), ACT.Copy,
                                     scale=M["colh"][:, 1, c:c + 1])
                if c < NCK - 1:
                    A.done(ins)
                else:
                    ins.then_inc(free[T(4) % 2], 1)
            act.wait_ge(head_loaded, 64 + 64 * h)
            for b in range(NS):
                ins = act.activation(M["cs"][:, b, :], M["cs"][:, b, :], ACT.Copy,
                                     scale=M["bc"][:, 1, SEQ + b:SEQ + b + 1])
                if b < NS - 1:
                    A.done(ins)
                else:
                    ins.then_inc(cs_scaled, 1)
            act.wait_ge(samp_var, 1 + h)
            act.activation(M["sv"][:, 1, :], M["sv"][:, 0, :], ACT.Sqrt).then_inc(samp_dev, 1)
            for c in range(NCK):
                if c < NCK - 1:
                    act.wait_ge(h_full, c + 1 + 7 * h)
                else:
                    fl(act, T(9), h, TPH)
                act.activation(M["hs"][:, c, :], flat(T(9), DV + 1, 512 * (c % 2)), ACT.Copy)\
                   .then_inc(h_free, 1)
            act.wait_ge(hs_ready, 1 + 2 * h)
            for c in range(NCK):
                A.done(act.activation(M["squares"][:, c, :], M["hs"][:, c, 0:DV], ACT.Square,
                                      accum_out=M["hv"][:, 0, c:c + 1]))
            A.sync()
            act.sem_inc(hsq_ready, 1)
            evac(10, M["so"][:, 0, :], ACT.Sigmoid)
            evac(11, M["so"][:, 1, :], ACT.Sigmoid)
            act.wait_ge(hvar_ready, 1 + h)
            act.activation(M["hv"][:, 2, :], M["hv"][:, 1, :], ACT.Sqrt).then_inc(hdev_ready, 1)
            for j in range(2):
                act.wait_ge(of_ready, j + 1 + 2 * h)
                act.activation(M["oh"][:, j, :], M["of"][:, j, :], ACT.Copy).then_inc(oh_ready, 1)

    def dve_mlstm(S, M):
        dve = nc.vector
        gate_rows(S, M)
        ev(dve, T_COLS)
        with S.loop(0, HEADS, M["dve_per"]) as h:
            T = lambda k: T_HEAD + k
            bc, colh, caug, cs, ns = M["bc"], M["colh"], M["caug"], M["cs"], M["ns"]
            dve.wait_ge(head_loaded, 64 + 64 * h)
            S.link(dve.tensor_copy(colh[:, :, :], M["cols"][:, bass.ds(h, 1), :, :]))
            S.done(dve.memset(M["va"][:, :, DV:DV + 1], 1.0))
            dve.memset(caug[:, :], 0.0).then_inc(c_upd, 1)
            for c in range(NCK):
                ins = dve.scalar_tensor_tensor(M["dm"][:, c, :], bc[:, 0, c * P:(c + 1) * P],
                                               colh[:, 0, c:c + 1], M["cmask"][:, :], ALU.add, ALU.min)
                if c < NCK - 1:
                    S.done(ins)
                else:
                    ins.then_inc(dm_ready, 1)
            ev(dve, T(0), h, TPH)
            dve.tensor_tensor(M["qw"][:, :], M["qT"][:, 0:SEQ], bc[:, 1, 0:SEQ], ALU.mult)\
               .then_inc(qw_ready, 1)
            ev(dve, T(1), h, TPH)
            q_s, k_s = M["qT"][:, SEQ:NT], M["kT"][:, SEQ:NT]
            S.done(dve.tensor_tensor(M["kiw"][:, :], k_s, bc[:, 0, SEQ:NT], ALU.mult))
            S.link(dve.tensor_tensor(ns[:, :], ns[:, :], bc[:, 1, SEQ:NT], ALU.mult))
            S.link(dve.tensor_tensor(ns[:, :], ns[:, :], M["kiw"][:, :], ALU.add))
            S.done(dve.tensor_tensor(M["prod"][:, :], ns[:, :], q_s, ALU.mult))
            for j in range(2):
                fl(dve, T(5 + j), h, TPH)
                dve.tensor_copy(M["va"][:, :, j * P:(j + 1) * P],
                                flat(T(5 + j), SEQ).rearrange("p (c n) -> p c n", n=P))\
                   .then_inc(free[T(5 + j) % 2], 1)
            fl(dve, T(7), h, TPH)
            dve.wait_ge(decay_ready, 1 + h)
            dve.tensor_tensor(M["p"][:, :], flat(T(7), SEQ), M["dm"][:, :, :].rearrange("p c n -> p (c n)"),
                              ALU.mult).then_inc(free[T(7) % 2], 1)
            dve.wait_ge(samp_pe, 1 + 4 * h)
            dve.tensor_copy(M["vs"][:, :], flat(T(8), DV, 1024)[0:NS]).then_inc(samp_dve, 1)
            dve_ada_rows(G_HEAD, 6, h, GPH)
            dve.wait_ge(cs_scaled, 1 + h)
            for g in range(2):
                dve.wait_ge(samp_pe, 2 + g + 4 * h)
                for b in range(4):
                    bb = 4 * g + b
                    ins = dve.scalar_tensor_tensor(cs[:, bb, :], flat(T(8), DV, b * DV),
                                                   M["kiw"][:, bb:bb + 1], cs[:, bb, :], ALU.mult, ALU.add)
                    if b < 3:
                        S.done(ins)
                    else:
                        ins.then_inc(samp_dve, 1)
            S.sync()
            dve.sem_inc(samp_dve, 1)
            dve.wait_ge(samp_pe, 4 + 4 * h)
            sd, sh = M["sd"], M["sh"]
            S.link(dve.tensor_copy(sd[:, 1, :], flat(T(8), NS, 1024)))
            S.link(dve.scalar_tensor_tensor(sd[:, 0, :], sd[:, 1, :], -1.0, sd[:, 1, :], ALU.mult, ALU.max))
            S.link(dve.tensor_tensor(sd[:, 0, :], sd[:, 0, :], M["bs"][:, :], ALU.max))
            S.link(dve.reciprocal(sd[:, 1, :], sd[:, 0, :]))
            S.link(dve.tensor_tensor(sh[:, :, :], flat(T(8), 2 * NS, 1024 + NS)
                                     .rearrange("p (j b) -> p j b", b=NS),
                                     sd[:, 1:2, :].to_broadcast([P, 2, NS]), ALU.mult))
            dve.tensor_tensor(M["sq2"][:, :, :], sh[:, :, :], sh[:, :, :], ALU.mult).then_inc(samp_dve, 1)
            fl(dve, T(8), h, TPH)
            dve.tensor_scalar(M["sv"][:, 0, :], flat(T(8), NS, 1024 + 64), 1.0 / DV, EPS, ALU.mult, ALU.add)\
               .then_inc(samp_var, 1)
            dve.wait_ge(samp_dev, 1 + h)
            dve.reciprocal(sd[:, 1, :], M["sv"][:, 1, :]).then_inc(free[T(8) % 2], 1)
            dve_ada(G_HEAD, 6, h, GPH)
            for c in range(NCK):
                if c == 4:
                    dve_ada_rows(G_HEAD + 1, 7, h, GPH)
                if c == 5:
                    dve_ada(G_HEAD + 1, 7, h, GPH)
                dve.wait_ge(c_full, c + 1 + 8 * h)
                dve.wait_ge(c_upd, c + 1 + 8 * h)
                if c < NCK - 1:
                    dve.wait_ge(h_full, c + 1 + 7 * h)
                else:
                    fl(dve, T(9), h, TPH)
                    dve.wait_ge(h_free, NCK + 8 * h)
                w = bc[:, 1, (c + 1) * P - 1:(c + 1) * P]
                dve.scalar_tensor_tensor(caug[:, :], caug[:, :], w, flat(T(9), DV + 1, 1024),
                                         ALU.mult, ALU.add)\
                   .then_inc(c_upd if c < NCK - 1 else free[T(9) % 2], 1)
            dve_ada_rows(G_HEAD + 2, 6, h, GPH)
            hs, hd, hv = M["hs"], M["hd"], M["hv"]
            S.link(dve.scalar_tensor_tensor(hd[:, 0, :], hs[:, :, DV], -1.0, hs[:, :, DV], ALU.mult, ALU.max))
            S.link(dve.tensor_tensor(hd[:, 0, :], hd[:, 0, :], colh[:, 2, :], ALU.max))
            S.link(dve.reciprocal(hd[:, 1, :], hd[:, 0, :]))
            dve.tensor_tensor(hs[:, :, 0:DV], hs[:, :, 0:DV],
                              hd[:, 1, :].unsqueeze(2).to_broadcast([P, NCK, DV]), ALU.mult)\
               .then_inc(hs_ready, 1)
            dve.wait_ge(hsq_ready, 1 + h)
            dve.tensor_scalar(hv[:, 1, :], hv[:, 0, :], 1.0 / DV, EPS, ALU.mult, ALU.add)\
               .then_inc(hvar_ready, 1)
            dve.wait_ge(hdev_ready, 1 + h)
            S.link(dve.reciprocal(hd[:, 0, :], hv[:, 2, :]))
            dve.tensor_tensor(hs[:, :, 0:DV], hs[:, :, 0:DV],
                              hd[:, 0, :].unsqueeze(2).to_broadcast([P, NCK, DV]), ALU.mult)\
               .then_inc(hs_ready, 1)
            S.link(dve.tensor_tensor(sh[:, :, :], sh[:, :, :], sd[:, 1:2, :].to_broadcast([P, 2, NS]), ALU.mult))
            S.link(dve.tensor_copy(M["ghl"][:, :], M["gh"][:, bass.ds(h, 1), :]))
            dve_ada(G_HEAD + 2, 6, h, GPH)
            ev(dve, T(11), h, TPH)
            for j in range(2):
                of = M["of"]
                S.done(dve.scalar_tensor_tensor(of[:, j, SEQ:NT], sh[:, j, :], M["ghl"][:, j:j + 1],
                                                M["so"][:, j, SEQ:NT], ALU.mult, ALU.mult))
                fl(dve, T(12 + j), h, TPH)
                dve.scalar_tensor_tensor(of[:, j, 0:SEQ], flat(T(12 + j), SEQ), M["ghl"][:, j:j + 1],
                                         M["so"][:, j, 0:SEQ], ALU.mult, ALU.mult)\
                   .then_inc(free[T(12 + j) % 2], 1)
                ev(dve, T(12 + j), h, TPH)
                S.sync()
                dve.sem_inc(of_ready, 1)
            for j in range(2):
                dve.wait_ge(oh_ready, j + 1 + 2 * h)
                dve.tensor_tensor(M["ol"][:, j, :], M["of"][:, j, :], M["oh"][:, j, :].bitcast(F32),
                                  ALU.subtract).then_inc(hho_ready, 1)
            dve.sem_inc(head_free, 1)
            dve.wait_ge(a_free, G_HEAD + GPH + h * GPH)
            dve_add_down(T(14), h, TPH, GT1, M["tmp"])

    HALVES = [(0, 512), (512, 1024)]
    GROUPS = [(n, k0, min(4, n % 8 + 1 - k0)) for n in range(16) for k0 in range(0, n % 8 + 1, 4)]
    NG = len(GROUPS)

    def pool_mla():
        for k in range(3):
            split_unit(U_DKV + k, 0, 0, T_FF0 + FF_FILLS - 1 if k < 2 else T_FF0 + FF_FILLS - 1, 0)
        for k in range(3):
            split_unit(U_DQ + k, 0, 0, T_DKV + k, 0)
        fl(nc.gpsimd, T_DQ + 2)
        used = [TK, TV, TP1 + TK, TP1 + TV, 49, 49]
        with nc.gpsimd.Fori(0, 4) as i:
            for k in range(UPP):
                f = used[k - 3] if k >= 3 else used[k + 3] - TPP
                split_unit(U_PAIR + k, i, UPP, T_PAIR + f, TPP, 2 if k in (1, 3) else KT)

    def sp_mla():
        for k in range(3):
            load_unit(U_DKV + k)
        for k in range(3):
            load_unit(U_DQ + k)
        with nc.sync.Fori(0, 4) as i:
            for k in range(UPP):
                load_unit(U_PAIR + k, i, UPP, 2 if k in (1, 3) else KT)

    def pe_latent(B, L):
        for n, u, T in ((2, U_DKV, T_DKV), (3, U_DQ, T_DQ)):
            for k in range(3):
                pe_up(u + k, 0, 0, T + k, 0, B["hnh"], B["hnl"], 9 * n + 2 if k == 0 else None)
        pe = nc.tensor
        for r, T, sums in ((3, T_CKN, L["ck_sum"]), (4, T_QN, L["cq_sum"])):
            pe.wait_ge(ss_ready, r + 1)
            take(T)
            for a, b in SUMS:
                mm = pe.matmul(flat(T, b - a, a), ones[:, :], sums[:, a:b], start=True, stop=True)
            mm.then_inc(full, 1)

    def latent_squares(S, T, raw_, tiles, sums, two):
        dve = nc.vector
        for k in range(tiles):
            ev(dve, T + k)
        S.done(dve.tensor_tensor(two, raw_[:, 1, :], raw_[:, 1, :], ALU.mult))
        S.link(dve.tensor_tensor(sums, raw_[:, 0, :], raw_[:, 0, :], ALU.mult))
        S.link(dve.tensor_tensor(sums, sums, two, ALU.add))
        if tiles == 3:
            S.link(dve.tensor_tensor(two, raw_[:, 2, :], raw_[:, 2, :], ALU.mult))
            S.link(dve.tensor_tensor(sums, sums, two, ALU.add))
        dve.sem_inc(ss_ready, 1)

    def latent_split(S, T, raw_, tiles, gcol, rstd, xh, xl, first):
        dve = nc.vector
        ev(dve, T)
        S.link(dve.reciprocal(rstd, rstd))
        for k in range(tiles):
            dve.scalar_tensor_tensor(raw_[:, k, :], raw_[:, k, :], gcol(k), rstd, ALU.mult, ALU.mult)\
               .then_inc(lat_ready, 1)
        for k in range(tiles):
            dve.wait_ge(lat_head, first + k + 1)
            S.done(dve.tensor_tensor(xl[:, k, :], raw_[:, k, :], xh[:, k, :].bitcast(F32), ALU.subtract))
        S.sync()
        dve.sem_inc(lat_split, 1)

    def act_latent_raw(T, raw_, tiles):
        act = nc.scalar
        for k in range(tiles):
            fl(act, T + k)
            act.activation(raw_[:, k, :].rearrange("p (c n) -> p c n", n=CH), slot(T + k), ACT.Copy)\
               .then_inc(free[(T + k) % 2], 1)

    def act_latent_head(T, raw_, tiles, std, xh, first):
        act = nc.scalar
        act_std(T, tiles * P, std)
        for k in range(tiles):
            act.wait_ge(lat_ready, first + k + 1)
            act.activation(xh[:, k, :], raw_[:, k, :], ACT.Copy).then_inc(lat_head, 1)

    def dve_latent(S, B, L):
        dve = nc.vector
        T = T_DKV + 2
        cos, sin, ta, tb = L["cos"], L["sin"], L["ta0"], L["tb0"]
        c3 = lambda a: a.rearrange("p (c n) -> p c n", n=CH)
        fl(dve, T)
        S.done(dve.tensor_tensor(c3(ta[64:96, :]), slot(T)[64:96], c3(cos[64:96, :]), ALU.mult))
        dve.tensor_tensor(c3(tb[64:96, :]), slot(T)[96:128], c3(sin[96:128, :]), ALU.mult)\
           .then_inc(free[T % 2], 1)
        ev(dve, T)
        S.sync()
        S.link(dve.tensor_tensor(L["kpr"][64:96, :], ta[64:96, :], tb[64:96, :], ALU.add))
        S.done(dve.tensor_copy(L["kps"][:, :], L["kpr"][64:96, SEQ:NT]))
        dve_norm_out(3, T_N2, 2, MODL + SC1, MODL + SH1, B, S, T_DKV + 2, keep=True)
        dve.wait_ge(hn_ready, 9 * 4)
        latent_squares(S, T_DKV, L["ckr"], 2, L["ck_sum"], L["sqt"])
        latent_squares(S, T_DQ, L["cqr"], 3, L["cq_sum"], L["sqt"])
        latent_split(S, T_CKN, L["ckr"], 2, lambda k: gn[:, 5, k:k + 1], L["ck_sum"],
                     L["ckh"], L["ckl"], 0)
        S.link(dve.tensor_copy(L["cks"][:, :, :], L["ckr"][:, :, SEQ:NT]))
        dve.sem_inc(latent_out, 1)
        latent_split(S, T_QN, L["cqr"], 3, lambda k: gn[:, 5, 2 + k:3 + k], L["cq_sum"],
                     L["cqh"], L["cql"], 2)

    def pe_attention(L, N):
        pe = nc.tensor
        ckh, ckl, cqh, cql = L["ckh"], L["ckl"], L["cqh"], L["cql"]
        pe.wait_ge(lat_split, 2)
        with pe.Fori(0, 4) as i:
            for pp in range(2):
                T = lambda k: T_PAIR + 21 * pp + k
                u = U_PAIR + 2 * pp
                pe.wait_ge(w_split, u + 1 + i * UPP)
                s = ring(u)
                for part in range(2):
                    take(T(TQ + part), i, TPP)
                    for kt in range(3):
                        mm = products(lambda c: flat(T(TQ + part), 512 if c < 2 else NS, 512 * c),
                                      hi[s][:, 3 * part + kt, :], lo[s][:, 3 * part + kt, :],
                                      cqh[:, kt, :], cql[:, kt, :], HALVES + [(SEQ, NT)],
                                      kt == 0, kt == 2)
                    mm.then_inc(full, 1)
                take(T(TK), i, TPP)
                for kt in range(2):
                    mm = products(lambda c: flat(T(TK), 512, 512 * c), hi[s][:, 6 + kt, :],
                                  lo[s][:, 6 + kt, :], ckh[:, kt, :], ckl[:, kt, :], HALVES,
                                  kt == 0, kt == 1)
                mm.then_inc(full, 1)
                s = ring(u + 1)
                pe.wait_ge(w_split, u + 2 + i * UPP)
                take(T(TV), i, TPP)
                for j in range(NCK):
                    tk = slice(j * P, (j + 1) * P)
                    for kt in range(2):
                        for p_, (a, b) in enumerate(((ckh, hi), (ckh, lo), (ckl, hi))):
                            mm = pe.matmul(flat(T(TV), P, j * P), a[:, kt, tk], b[s][:, kt, :],
                                           start=(kt + p_ == 0), stop=(kt == 1 and p_ == 2))
                mm.then_inc(full, 1)
                ev(pe, T(TK), i, TPP)
                pe.wait_ge(q_ready, 1 + pp + 2 * i)
                pair = lambda n: n + pp * 16

                def scores(n):
                    e, qt = n // 8, n % 8
                    take(T(4 + n), i, TPP)
                    w = (qt + 1) * P
                    for c in range(0, w, 512):
                        mm = pe.matmul(flat(T(4 + n), min(512, w - c), c),
                                       N["q"][0:96, e, qt * P:(qt + 1) * P],
                                       N["k"][0:96, e, c:min(w, c + 512)], start=True, stop=True)
                    mm.then_inc(full, 1)

                def turn(n):
                    ev(pe, T(4 + n), i, TPP)
                    for g, (gn_, k0, m) in enumerate(GROUPS):
                        if gn_ == n:
                            if g >= 2:
                                pe.wait_ge(pt_copied[g % 2], g // 2 + pp * NG // 2 + i * NG)
                            for k in range(m):
                                mm = pe.transpose(ps[:, 6 + g % 2, k * P:(k + 1) * P],
                                                  N["pex"][:, n % 2, (k0 + k) * P:(k0 + k + 1) * P],
                                                  ident[:, :])
                            mm.then_inc(pt_full[g % 2], 1)

                def values(n):
                    e, qt = n // 8, n % 8
                    if n >= 2:
                        pe.wait_ge(o_free, pair(n - 1) + 32 * i)
                    if n == 0:
                        ev(pe, T(TV), i, TPP)
                    o = ps[:, 2 + 3 * (n % 2), 0:64]
                    for g, (gn_, k0, m) in enumerate(GROUPS):
                        if gn_ == n:
                            pe.wait_ge(pt_copied[g % 2], g // 2 + 1 + pp * NG // 2 + i * NG)
                            for k in range(m):
                                mm = pe.matmul(o, N["pt"][:, g % 4, k * P:(k + 1) * P],
                                               N["v"][:, k0 + k, e * 64:(e + 1) * 64],
                                               start=(k0 + k == 0), stop=(k0 + k == qt))
                    mm.then_inc(o_full, 1)

                scores(0)
                for n in range(17):
                    if n < 15:
                        scores(n + 1)
                    if n < 16:
                        turn(n)
                    if n:
                        values(n - 1)
                pe.wait_ge(o_free, pair(16) + 32 * i)
                take(T(20), i, TPP)
                for qt in range(NCK):
                    mm = pe.transpose(flat(T(20), P, qt * P), N["att"][:, qt, :], ident[:, :])
                mm.then_inc(full, 1)
            T = lambda k: T_PAIR + k
            pe.wait_ge(w_split, U_PAIR + 6 + i * UPP)
            ev(pe, T(41), i, TPP)
            for m in range(KT):
                take(T(42 + m), i, TPP)
                for pp in range(2):
                    s = ring(U_PAIR + 4 + pp)
                    mm = products(lambda c: flat(T(42 + m), 512, 512 * c), hi[s][:, m, :], lo[s][:, m, :],
                                  N["ath"][:, pp, :], N["atl"][:, pp, :], HALVES, pp == 0, pp == 1)
                mm.then_inc(full, 1)

    def act_attention(N):
        act = nc.scalar
        q, k_ = N["q"], N["k"]
        with A.loop(0, 4, N["act_per"]) as i:
            for pp in range(2):
                T = lambda k: T_PAIR + 21 * pp + k
                fl(act, T(TQ), i, TPP)
                for e in range(2):
                    A.done(act.activation(q[0:64, e, :], flat(T(TQ), SEQ)[64 * e:64 * e + 64], ACT.Copy,
                                          scale=ATT_SCALE))
                    ins = act.activation(N["qsn"][:, bass.ds(4 * i + 2 * pp + e, 1), :],
                                         flat(T(TQ), NS, SEQ)[64 * e:64 * e + 64].unsqueeze(1),
                                         ACT.Copy, scale=ATT_SCALE)
                    if e:
                        ins.then_inc(free[T(TQ) % 2], 1)
                    else:
                        A.done(ins)
                fl(act, T(TK), i, TPP)
                A.done(act.activation(k_[0:64, 0, :], flat(T(TK), SEQ)[0:64], ACT.Copy))
                act.activation(k_[0:64, 1, :], flat(T(TK), SEQ)[64:128], ACT.Copy)\
                   .then_inc(free[T(TK) % 2], 1)
                pair = lambda n: n + pp * 16

                def exps(n):
                    w = (n % 8 + 1) * P
                    act.wait_ge(nm_ready, pair(n + 1) + 32 * i)
                    if n >= 2:
                        g = [j for j, gr in enumerate(GROUPS) if gr[0] == n - 2][-1]
                        act.wait_ge(pt_full[g % 2], g // 2 + 1 + pp * NG // 2 + i * NG)
                    act.activation(N["pex"][:, n % 2, 0:w], flat(T(4 + n), w), ACT.Exp,
                                   bias=N["nm"][:, n % 2:n % 2 + 1], accum_out=N["rs"][:, n % 4:n % 4 + 1])\
                       .then_inc(free[T(4 + n) % 2], 1)

                exps(0)
                for n in range(16):
                    if n < 15:
                        exps(n + 1)
                    copy_group(act, n, 0, i, pp, N)
                fl(act, T(20), i, TPP)
                act.activation(N["ath"][:, pp, :], flat(T(20), SEQ), ACT.Copy).then_inc(at_head, 1)

    def copy_group(eng, n, side, i, pp, N):
        for g, (gn_, k0, m) in enumerate(GROUPS):
            if gn_ == n and g % 2 == side:
                eng.wait_ge(pt_full[side], g // 2 + 1 + pp * NG // 2 + i * NG)
                if g >= 4:
                    eng.wait_ge(o_full, GROUPS[g - 4][0] + 1 + pp * 16 + 32 * i)
                dst, src = N["pt"][:, g % 4, 0:m * P], ps[:, 6 + side, 0:m * P]
                ins = eng.tensor_copy(dst, src) if side else eng.activation(dst, src, ACT.Copy)
                ins.then_inc(pt_copied[side], 1)

    def dve_attention(S, L, N):
        dve = nc.vector
        q, k_, ta, tb = N["q"], N["k"], N["ta"], N["tb"]
        for e in range(2):
            S.done(dve.tensor_copy(k_[64:96, e, :], L["kpr"][64:96, 0:SEQ]))
        with S.loop(0, 4, N["dve_per"]) as i:
            for pp in range(2):
                T = lambda k: T_PAIR + 21 * pp + k
                fl(dve, T(TR), i, TPP)
                S.done(dve.scalar_tensor_tensor(ta[:, :], flat(T(TR), NT)[0:64], ATT_SCALE,
                                                L["cos"][0:64, :], ALU.mult, ALU.mult))
                dve.scalar_tensor_tensor(tb[:, :], flat(T(TR), NT)[64:128], ATT_SCALE,
                                         L["sin"][64:128, :], ALU.mult, ALU.mult)\
                   .then_inc(free[T(TR) % 2], 1)
                ev(dve, T(TR), i, TPP)
                S.sync()
                for e in range(2):
                    r = slice(32 * e, 32 * e + 32)
                    S.done(dve.tensor_tensor(q[64:96, e, :], ta[r, 0:SEQ], tb[r, 0:SEQ], ALU.add))
                    S.done(dve.tensor_tensor(N["qsp"][:, bass.ds(4 * i + 2 * pp + e, 1), :],
                                             ta[r, SEQ:NT].unsqueeze(1), tb[r, SEQ:NT].unsqueeze(1),
                                             ALU.add))
                S.sync()
                dve.sem_inc(q_ready, 1)
                fl(dve, T(TV), i, TPP)
                dve.tensor_copy(N["v"][:, :, :].rearrange("p j c -> p (j c)"), flat(T(TV), SEQ))\
                   .then_inc(free[T(TV) % 2], 1)
                pair = lambda n: n + pp * 16

                def row_max(n):
                    qt = n % 8
                    fl(dve, T(4 + n), i, TPP)
                    d = flat(T(4 + n), P, qt * P)
                    S.link(dve.tensor_tensor(d, d, N["amask"][:, :], ALU.add))
                    dve.tensor_reduce(N["nm"][:, n % 2:n % 2 + 1], flat(T(4 + n), (qt + 1) * P), AX.X,
                                      ALU.max, negate=True).then_inc(nm_ready, 1)

                def out(n):
                    e, qt = n // 8, n % 8
                    ev(dve, T(4 + n), i, TPP)
                    S.link(dve.reciprocal(N["ri"][:, n % 2:n % 2 + 1], N["rs"][:, n % 4:n % 4 + 1]))
                    dve.wait_ge(o_full, pair(n + 1) + 32 * i)
                    dve.tensor_scalar(N["att"][:, qt, e * 64:(e + 1) * 64], ps[:, 2 + 3 * (n % 2), 0:64],
                                      N["ri"][:, n % 2:n % 2 + 1], None, ALU.mult).then_inc(o_free, 1)

                row_max(0)
                for n in range(17):
                    if n < 15:
                        row_max(n + 1)
                    if n < 16:
                        copy_group(dve, n, 1, i, pp, N)
                    if n:
                        out(n - 1)
                dve.wait_ge(at_head, 1 + pp + 2 * i)
                dve.tensor_tensor(N["atl"][:, pp, :], flat(T(20), SEQ), N["ath"][:, pp, :].bitcast(F32),
                                  ALU.subtract).then_inc(free[T(20) % 2], 1)
            for m in range(KT):
                T42 = T_PAIR + 42 + m
                fl(dve, T42, i, TPP)
                dve.scalar_tensor_tensor(x[:, m, 0:SEQ], flat(T42, SEQ), mod[:, MODL + GT1 + m, 0:1],
                                         x[:, m, 0:SEQ], ALU.mult, ALU.add).then_inc(free[T42 % 2], 1)

    def sp_samples(Z):
        sp = nc.sync

        def load(b, j):
            for g in range(NCK):
                page = sp.value_load(Z["pt"][0:1, bass.ds(b * NCK + g, 1)], min_val=0, max_val=t["n_phys"] - 1)
                sp.dma_start(Z["kc"][j][:, g, :], t["cache_ckv"][bass.ds(page, 1)]
                             .rearrange("a p c -> p (a c)")).then_inc(kv_loaded[j], 16)
                sp.dma_start(Z["kp"][j][:, g, :], t["cache_kpe"][bass.ds(page, 1)]
                             .rearrange("a p c -> p (a c)")).then_inc(kv_loaded[j], 16)

        last = T_PAIR + 3 * TPP + TP1
        ev(sp, last + TR)
        fl(sp, last + TV)
        sp.dma_start(Z["pt"][:, :], t["page_table"]).then_inc(pages_in, 16)
        sp.wait_ge(pages_in, 16)
        for j in range(2):
            load(j, j)
        fl(sp, T_PAIR + 4 * TPP - 1)
        sp.dma_start(Z["wuk"][:, :, :], t["w_ukT"]).then_inc(samp_w, 16)
        sp.dma_start(Z["wuv"][:, :, :], t["w_uv"]).then_inc(samp_w, 16)
        for j in range(2, 4):
            load(j, j)
        with sp.Fori(1, NS // 4) as i:
            for j in range(4):
                sp.wait_ge(z_ol, 4 * i + j - 3)
                load(4 * i + j, j)

    Z_OT = P + MH
    Z_OL = Z_OT + 2 * MH
    KVL16 = 16 * 2 * NCK

    TS = 4 * TPS

    def pe_two_sequences(hp, i, Z):
        pe = nc.tensor
        for j in range(2):
            T = lambda k: T_SAMP + 8 * hp + 3 * j + k
            kc, kp = Z["kc"][2 * hp + j], Z["kp"][2 * hp + j]
            pe.wait_ge(kv_loaded[2 * hp + j], KVL16 + KVL16 * i)
            for a in range(2):
                take(T(a), i, TS)
                for g in range(NCK):
                    if a == 1 and g == NCK - 1:
                        take(T(2), i, TS)
                    mm = pe.transpose(flat(T(a), P, g * P), kc[:, g, a * P:(a + 1) * P], ident[:, :])
                mm.then_inc(full, 1)
            for g in range(NCK):
                mm = pe.transpose(flat(T(2), P, g * P)[0:32], kp[:, g, :], ident[:, :])
            mm.then_inc(full, 1)
        for j in range(2):
            T = T_SAMP + 8 * hp + 6 + j
            pe.wait_ge(z_qb, 1 + j + 2 * hp + 4 * i)
            take(T, i, TS)
            if j == 0:
                ev(pe, T_SAMP + 8 * hp + 1, i, TS)
            cT, kT = Z["cT"][j], Z["kT"][j]
            for (c0, c1) in ((0, 512), (512, 1024), (1024, 1025)):
                o = flat(T, c1 - c0, c0)[0:MH]
                pe.matmul(o, Z["qb"][:, j, 0, :], cT[:, 0, c0:c1], start=True, stop=False)
                pe.matmul(o, Z["qb"][:, j, 1, :], cT[:, 1, c0:c1], start=False, stop=False)
                mm = pe.matmul(o, Z["qpb"][:, j, :], kT[:, c0:c1], start=False, stop=True)
            mm.then_inc(full, 1)
        for j in range(2):
            T, kc, pr = T_SAMP + 8 * hp + 6 + j, Z["kc"][2 * hp + j], Z["pr"][j]
            ev(pe, T, i, TS)
            for g in range(NCK):
                pe.matmul(ps[:, 6 + j, g * MH:(g + 1) * MH], pr[:, g * P:(g + 1) * P],
                          ident[0:MH, 0:MH], start=True, stop=True)
            mm = pe.matmul(ps[0:NS, 6 + j, P:P + MH], pr[:, SEQ:SEQ + 1].to_broadcast([MH, NS]),
                           ident[0:MH, 0:MH], start=True, stop=True)
            mm.then_inc(z_pt, 1)
        for j in range(2):
            kc, o = Z["kc"][2 * hp + j], ps[0:MH, 6 + j, Z_OL:Z_OL + KVL]
            pe.wait_ge(z_ptc, 1 + j + 2 * hp + 4 * i)
            for g in range(NCK):
                pe.matmul(o, Z["prT"][:, j, g, :], kc[:, g, :],
                          start=(g == 0), stop=False)
            mm = pe.matmul(o, Z["prn"][:, j, :], Z["ckt"][:, :], start=False, stop=True)
            mm.then_inc(z_ol, 1)
        for j in range(2):
            pe.wait_ge(z_olc, 1 + j + 2 * hp + 4 * i)
            for a in range(2):
                o = Z_OT + a * MH
                mm = pe.matmul(ps[:, 6 + j, o:o + MH], Z["ol"][:, j, a * P:(a + 1) * P],
                               ident[0:MH, 0:MH], start=True, stop=True)
            mm.then_inc(z_ot, 1)

    def pe_samples(Z, L, N):
        pe = nc.tensor
        for j in range(2):
            mm = pe.transpose(ps[0:NS, 7, j * P:(j + 1) * P], L["cks"][:, j, :], ident[:, :])
        mm.then_inc(z_pe, 1)
        pe.wait_ge(samp_w, 32)
        pe.wait_ge(z_dve, 1)
        for h in range(MH):
            for j in range(2):
                mm = pe.matmul(ps[:, 6, (j * MH + h) * NS:(j * MH + h + 1) * NS],
                               Z["wuk"][:, h, j * P:(j + 1) * P], N["qsn"][:, h, :], start=True, stop=True)
        mm.then_inc(z_pe, 1)
        with pe.Fori(0, NS // 4) as i:
            for hp in range(2):
                pe_two_sequences(hp, i, Z)
        pe.wait_ge(kv_used, NS)
        for p_ in range(8):
            for a in range(2):
                mm = pe.matmul(ps[:, 7, p_ * 16:p_ * 16 + 16], Z["wuv"][:, a, p_ * P:(p_ + 1) * P],
                               Z["olT"][:, a, 2 * p_:2 * p_ + 2, :].rearrange("p h b -> p (h b)"),
                               start=(a == 0), stop=(a == 1))
        mm.then_inc(z_pe, 1)
        pe.wait_ge(z_dve, 2)
        for m in range(KT):
            u = NMOD + m
            pe.wait_ge(a_loaded[u % 2], (u // 2 + 1) * 16)
            for kt in range(KT):
                mm = pe.matmul(ps[:, 6, m * NS:(m + 1) * NS], araw[u % 2][:, kt, :], Z["at"][:, kt, :],
                               start=(kt == 0), stop=(kt == KT - 1))
            mm.then_inc(a_used, 1)

    def act_samples(Z):
        act = nc.scalar
        c = lambda T, a, i, dst, src: (fl(act, T, i, TS),
                                       act.activation(dst, src, ACT.Copy).then_inc(free[T % 2], 1))
        with act.Fori(0, NS // 4) as i:
            for hp in range(2):
                for j in range(2):
                    T = lambda k: T_SAMP + 8 * hp + 3 * j + k
                    for a in range(2):
                        c(T(a), a, i, Z["cT"][j][:, a, 0:SEQ], flat(T(a), SEQ))
                    c(T(2), 2, i, Z["kT"][j][:, 0:SEQ], flat(T(2), SEQ)[0:32])
                for j in range(2):
                    T = T_SAMP + 8 * hp + 6 + j
                    act.wait_ge(z_nm, 1 + j + 2 * hp + 4 * i)
                    act.activation(Z["pr"][j][:, :], flat(T, SEQ + 1)[0:MH], ACT.Exp, bias=Z["nm"][:, j:j + 1],
                                   accum_out=Z["rs"][:, j:j + 1]).then_inc(free[T % 2], 1)

    def dve_samples(S, Z, L, N):
        dve = nc.vector
        dve.wait_ge(z_pe, 1)
        S.link(dve.tensor_copy(Z["ckt"][:, :], ps[0:NS, 7, 0:KVL]))
        dve.sem_inc(z_dve, 1)
        dve.wait_ge(z_pe, 2)
        S.link(dve.tensor_copy(Z["ql"][:, :, :, :], ps[:, 6, 0:KVL].rearrange("p (a h b) -> p a b h", a=2, h=MH)))
        with S.loop(0, NS // 4, Z["dve_per"]) as i:
            for hp in range(2):
                for j in range(2):
                    b = 4 * i + 2 * hp + j
                    S.done(dve.tensor_copy(Z["qb"][:, j, :, :].unsqueeze(2), Z["ql"][:, :, bass.ds(b, 1), :]))
                    S.done(dve.tensor_copy(Z["qpb"][:, j, :].unsqueeze(2), N["qsp"][:, :, bass.ds(b, 1)]))
                    S.done(dve.tensor_copy(Z["cT"][j][:, :, SEQ:SEQ + 1], L["cks"][:, :, bass.ds(b, 1)]))
                    S.done(dve.tensor_copy(Z["kT"][j][:, SEQ:SEQ + 1], L["kps"][:, bass.ds(b, 1)]))
                    S.sync()
                    dve.sem_inc(z_qb, 1)
                for j in range(2):
                    T = T_SAMP + 8 * hp + 6 + j
                    fl(dve, T, i, TS)
                    dve.tensor_reduce(Z["nm"][:, j:j + 1], flat(T, SEQ + 1)[0:MH], AX.X, ALU.max, negate=True)\
                       .then_inc(z_nm, 1)
                for j in range(2):
                    dve.wait_ge(z_pt, 1 + j + 2 * hp + 4 * i)
                    S.done(dve.tensor_copy(Z["prT"][:, j, :, :].rearrange("p g h -> p (g h)"),
                                           ps[:, 6 + j, 0:P]))
                    S.link(dve.tensor_scalar(Z["prn"][:, j, :], ps[0:NS, 6 + j, P:P + MH],
                                             ident[0:NS, bass.ds(4 * i + 2 * hp + j, 1)], None, ALU.mult))
                    dve.sem_inc(z_ptc, 1)
                    ev(dve, T_SAMP + 8 * hp + 6 + j, i, TS)
                    S.link(dve.reciprocal(Z["ri"][:, j:j + 1], Z["rs"][:, j:j + 1]))
                for j in range(2):
                    dve.wait_ge(z_ol, 1 + j + 2 * hp + 4 * i)
                    dve.tensor_scalar(Z["ol"][:, j, :], ps[0:MH, 6 + j, Z_OL:Z_OL + KVL], Z["ri"][:, j:j + 1],
                                      None, ALU.mult).then_inc(z_olc, 1)
                for j in range(2):
                    dve.wait_ge(z_ot, 1 + j + 2 * hp + 4 * i)
                    dve.tensor_copy(Z["olT"][:, :, :, bass.ds(4 * i + 2 * hp + j, 1)],
                                    ps[:, 6 + j, Z_OT:Z_OL].rearrange("p (a h o) -> p a h o", a=2, o=1))\
                       .then_inc(kv_used, 1)
        dve.wait_ge(z_pe, 3)
        v = ps[:, 7, 0:P].rearrange("p (k e b) -> p k e b", e=2, b=NS)
        for e in range(2):
            r = slice(64 * e, 64 * e + 64)
            S.done(dve.tensor_copy(Z["at"][r, :, :], v[r, :, e, :]))
        S.sync()
        dve.sem_inc(z_dve, 1)
        dve.wait_ge(a_used, NMOD + KT)
        S.link(dve.tensor_tensor(nsm[:, :, :], ps[:, 6, 0:KT * NS].rearrange("p (k b) -> p k b", b=NS),
                                 mod[:, MODL + GT1:MODL + GT1 + KT, 1:NC9], ALU.mult))
        dve.tensor_tensor(x[:, :, SEQ:NT], x[:, :, SEQ:NT], nsm[:, :, :], ALU.add).then_inc(x_done, 1)

    block = ctx.enter_context(nc.Block())

    @block.sync
    def _(sp):
        for dst, name in ((sc, "c"), (b_ada, "b_ada"), (gn, "gains"), (ident, "ident"), (cmask, "cmask"),
                          (reset, "reset"), (gf, "g_final"), (gh, "g_head"), (bg, "b_gates"), (m0, "state_m")):
            sp.dma_start(dst[tuple(slice(None) for _ in dst.shape)], t[name]).then_inc(s_const, 16)
        for k in range(KT):
            sp.dma_start(x[:, k, :], t["x"][:, k, :]).then_inc(x_loaded, 16)
        load_unit(0)
        for u in range(4 * G_HEAD):
            load_ada(u)
        sp_mlstm(M)
        for l, (n, F, U) in enumerate(((1, F0, U_FF0), (4, F1, U_FF1))):
            if l == 1:
                sp_mla()
                sp_samples(Z)
                for m in range(KT):
                    load_ada(NMOD + m)
            sp_ffn(U, G_FF if l == 0 else None, l, F)
            sp.wait_ge(co_ready, l + 1)
            sp.dma_start(t["conv_out"][l], F["co"][:, :, :]).then_inc(out_done, 16)
            sp.dma_start(t["conv_prev"][l], F["cb"][:, :, 1, :]).then_inc(out_done, 16)
            if l == 0:
                sp.wait_ge(out_done, 64)
                sp.dma_start(L["cos"][:, :], t["cos"]).then_inc(tables_in, 16)
                sp.dma_start(L["sin"][:, :], t["sin"]).then_inc(tables_in, 16)
        for k in range(KT):
            sp.wait_ge(y_ready, k + 1)
            sp.dma_start(t["y"][:, k, :], yb[:, k, :]).then_inc(y_out, 16)
        sp.wait_ge(y_out, 16 * KT)
        sp.wait_ge(out_done, 16 * 8)
        sp.wait_ge(head_out, 64 * HEADS)

    @block.gpsimd
    def _(pool):
        pool.wait_ge(ones_ready, 2)
        pool_sum_squares(0, B0)
        pool_mlstm()
        pool_sum_squares(1, B1)
        pool_ffn(U_FF0, T_FF0, T_N1 - 1)
        pool_sum_squares(2, B2)
        pool_mla()
        pool_sum_squares(3, B3)
        pool_ffn(U_FF1, T_FF1, T_PAIR + 4 * TPP - 1)
        pool_sum_squares(4, F1)

    @block.scalar
    def _(act):
        act.wait_ge(s_const, 10 * 16)
        act.wait_ge(ones_ready, 2)
        act.activation(sc[:, :, :], sc[:, :, :], ACT.Silu).then_inc(silu_ready, 1)
        act_squares(0, x_in, B0)
        act_std(T_N0, D, B0["rstd"][:, :])
        act_norm_out(0, SH1, B0)
        act_mlstm(M)
        act_squares(1, x_added(27), B1)
        act_std(T_N1, D, F0["rstd"][:, :])
        act_norm_out(1, SH2, F0)
        act_ffn(1, 0, T_FF0, F0)
        act_squares(2, x_added(126), B2)
        act.wait_ge(out_done, 16 * 4)
        act_std(T_N2, D, BL["rstd"][:, :])
        act_norm_out(2, SHKV, BL)
        act_latent_raw(T_DKV, L["ckr"], 2)
        act_norm_out(3, MODL + SH1, BL, T_DKV + 2)
        act_latent_raw(T_DQ, L["cqr"], 3)
        act_latent_head(T_CKN, L["ckr"], 2, L["ck_sum"], L["ckh"], 0)
        act_latent_head(T_QN, L["cqr"], 3, L["cq_sum"], L["cqh"], 2)
        act.wait_ge(latent_out, 1)
        act.dma_start(t["ckv_out"], L["ckr"][:, :, :]).then_inc(out_done, 16)
        act.dma_start(t["kpe_out"], L["kpr"][64:96, :]).then_inc(out_done, 16)
        act.dma_start(N["amask"][:, :], t["amask"]).then_inc(tables_in, 16)
        act.wait_ge(out_done, 16 * 6)
        act_attention(N)
        act_samples(Z)
        act_squares(3, lambda k: ev(act, T_PAIR + 42 + k + 3 * TPP) if k < KT else act.wait_ge(x_done, 136), B3)
        act_std(T_N3, D, F1["rstd"][:, :])
        act_norm_out(4, MODL + SH2, F1)
        act_ffn(4, 1, T_FF1, F1)
        act_squares(4, x_added(226), F1)
        act_std(T_N4, D, F1["rstd"][:, :])

    @block.tensor
    def _(pe):
        pe.wait_ge(s_const, 10 * 16)
        pe.wait_ge(ones_ready, 2)
        pe.wait_ge(silu_ready, 1)
        for g in range(G_HEAD):
            pe_ada_units(g, range(4), 6 + g % 2, before=g - 1 if g > 1 else None)
            if g:
                pe_ada_turn(g - 1, 6 + (g - 1) % 2)
        pe_ada_turn(G_HEAD - 1, 6 + (G_HEAD - 1) % 2)
        pe_total(0, 0, T_N0, B0)
        pe_mlstm(M)
        pe_total(1, 1, T_N1, B1)
        pe_ffn(1, U_FF0, T_FF0, F0, G_FF)
        pe_total(2, 2, T_N2, B2)
        pe_latent(BL, L)
        pe_attention(L, N)
        pe_samples(Z, L, N)
        pe_total(3, 5, T_N3, B3)
        pe_ffn(4, U_FF1, T_FF1, F1, None)
        pe_total(4, 6, T_N4, F1)

    @block.vector
    def _(dve):
        S = Steps(dve, dve_step)
        dve.memset(eps[:, :], EPS).then_inc(ones_ready, 1)
        dve.memset(ones[:, :], 1.0).then_inc(ones_ready, 1)
        dve.wait_ge(s_const, 10 * 16)
        for g in range(G_HEAD):
            dve_ada_rows(g, 6 + g % 2)
            if g:
                dve_ada(g - 1, 6 + (g - 1) % 2)
        dve_ada(G_HEAD - 1, 6 + (G_HEAD - 1) % 2)
        dve.wait_ge(a_free, G_HEAD)
        dve_sum_samples(0, B0)
        dve_norm_out(0, T_N0, 0, SC1, SH1, B0, S)
        dve_mlstm(S, M)
        dve_sum_samples(1, B1)
        dve_norm_out(1, T_N1, 1, SC2, SH2, F0, S)
        dve_ffn(S, 1, 0, T_FF0, F0, GT2, G_FF)
        dve.wait_ge(a_free, NMOD // 4)
        dve_sum_samples(2, B2)
        dve_norm_out(2, T_N2, 4, SCKV, SHKV, BL, S)
        dve.wait_ge(tables_in, 32)
        dve_latent(S, BL, L)
        dve.wait_ge(tables_in, 48)
        dve.wait_ge(out_done, 16 * 6)
        dve_attention(S, L, N)
        dve_samples(S, Z, L, N)
        dve_sum_samples(3, B3)
        dve_norm_out(4, T_N3, 3, MODL + SC2, MODL + SH2, F1, S)
        dve_ffn(S, 4, 1, T_FF1, F1, MODL + GT2, None)
        dve_sum_samples(4, F1)
        ev(dve, T_N4)
        S.link(dve.reciprocal(F1["rstd"][:, :], F1["rstd"][:, :]))
        for k in range(KT):
            dve.scalar_tensor_tensor(yb[:, k, :], x[:, k, :], gf[:, k:k + 1],
                                     F1["rstd"][:, :], ALU.mult, ALU.mult).then_inc(y_ready, 1)


_OUT = [("y", (128, 8, 1032)), ("C_prompt", (4, 128, 256)), ("n_prompt", (4, 128, 1)), ("m_prompt", (4, 1)),
        ("C_sample", (4, 8, 128, 256)), ("n_sample", (4, 128, 8)), ("m_sample", (4, 8)),
        ("conv_out", (2, 128, 22, 10)), ("conv_prev", (2, 128, 22, 8)), ("ckv_out", (128, 2, 1032)), ("kpe_out", (32, 1032))]


def kernel(**a):
    import numpy as _np
    import concourse.bacc as _bacc
    from concourse import mybir as _mybir
    from concourse.bass_utils import run_bass_kernel_spmd as _run

    a = {k: _np.asarray(v) for k, v in a.items()}
    f32 = _np.float32
    tr = _np.transpose

    def up(w):
        return tr(w.reshape(8, 128, -1, 128), (2, 1, 0, 3))

    def down(w):
        return w.reshape(-1, 128, 8, 128)

    def feat(v):
        v = v.reshape(v.shape[:-1] + (-1, 128))
        return tr(v, (v.ndim - 1, v.ndim - 2) + tuple(range(v.ndim - 2)))

    w_in = a["w_m_in"][0]
    wg = _np.zeros((1024, 128), f32)
    wg[:, 0:4], wg[:, 64:68] = w_in[:, 3072:3076], w_in[:, 3076:3080]
    units = [up(wg)]
    q, k, v, o = (up(w_in[:, s:e]) for s, e in ((0, 512), (512, 1024), (1024, 2048), (2048, 3072)))
    wo = down(a["w_m_out"][0])
    for h in range(4):
        units += [q[h:h + 1], k[h:h + 1], v[2 * h:2 * h + 2], o[2 * h:2 * h + 2], wo[2 * h:2 * h + 2]]

    def ffn(l):
        ug, dn = up(a["w_up"][l]), down(a["w_down"][l])
        out = []
        for r in range(11):
            a0, g0, a1, g1 = (ug[j:j + 1] for j in (2 * r, 22 + 2 * r, 2 * r + 1, 23 + 2 * r))
            out += [a0, g0] + ([dn[2 * r - 2:2 * r]] if r else []) + [a1, g1]
        return out + [dn[20:22]]

    units += ffn(0)
    wd = a["w_dkv"]
    kr = _np.zeros((1024, 128), f32)
    kr[:, 64:96] = wd[:, 256:288]
    kr[:, 96:112], kr[:, 112:128] = wd[:, 272:288], wd[:, 256:272]
    units += [up(wd[:, 0:256]), up(kr), up(a["w_dq"][0])]
    wuq = a["w_uq"][0].reshape(3, 128, 16, 96)
    wuk, wuv = a["w_uk"].reshape(2, 128, 16, 64), a["w_uv"].reshape(2, 128, 16, 64)
    w_o = down(a["w_o"][0])
    for i in range(4):
        for pp in range(2):
            hs = slice(4 * i + 2 * pp, 4 * i + 2 * pp + 2)
            n = wuq[:, :, hs, 0:64].reshape(3, 128, 128)
            r = wuq[:, :, hs, 64:96].reshape(3, 128, 64)
            s = _np.concatenate([wuq[:, :, hs, 80:96], wuq[:, :, hs, 64:80]], axis=3).reshape(3, 128, 64)
            r = _np.concatenate([r, s], axis=2)
            uk = wuk[:, :, hs].reshape(2, 128, 128)
            units.append(tr(_np.concatenate([n, r, uk], axis=0), (1, 0, 2))[None])
            uv = _np.zeros((1, 128, 8, 128), f32)
            uv[0, :, 0:2] = tr(wuv[:, :, hs].reshape(2, 128, 128), (1, 0, 2))
            units.append(uv)
        units.append(w_o[2 * i:2 * i + 2])
    units += ffn(1)
    def groups(w):
        return tr(w.reshape(4, 2, 128, -1, 512), (3, 0, 2, 1, 4)).reshape(-1, 128, 8, 128)

    ada = [groups(a["w_ada"][0]), groups(a["w_ada"][1]), groups(a["w_ada_kv"]), up(a["w_o"][0])]

    pos = _np.arange(1032).astype(f32)
    pos[1024:] = 1024
    freq = (f32(10000.0) ** (-_np.arange(16, dtype=f32) / f32(16))).astype(f32)
    row = _np.arange(128)
    ang = (freq[row % 16][:, None] * pos[None, :]).astype(f32)
    sign = _np.where(row % 32 < 16, -1.0, 1.0).astype(f32)[:, None]
    j = _np.arange(128)
    reset = _np.ones((4, 1024), f32)
    reset[:, ::128] = 0.0

    xs = _np.concatenate([a["x_prompt"][0], a["x_sample"][:, 0]], axis=0)
    gains = _np.zeros((128, 6, 8), f32)
    for n, g in enumerate((a["g_norm1"][0], a["g_norm2"][0], a["g_norm1"][1], a["g_norm2"][1], a["g_kv_in"])):
        gains[:, n] = feat(g)
    gains[:, 5, 0:2], gains[:, 5, 2:5] = feat(a["g_kv"]), feat(a["g_q"][0])
    conv_w = _np.concatenate([a["w_conv"], a["b_conv"][:, None]], axis=1)
    arrays = {
        "x": feat(xs), "c": feat(_np.concatenate([a["c_prompt"], a["c_sample"]], axis=0)),
        "w_units": _np.concatenate(units, axis=0), "ada_units": _np.concatenate(ada, axis=0),
        "b_ada": feat(_np.concatenate([a["b_ada"][0], a["b_ada"][1], a["b_ada_kv"]])),
        "gains": gains, "g_final": feat(a["g_final"]), "g_head": tr(a["g_m_head"][0].reshape(4, 2, 128), (2, 0, 1)),
        "b_gates": a["b_m_gates"][0].reshape(2, 4).T,
        "state_C": tr(a["state_mlstm_C"][0], (1, 0, 2, 3)), "state_n": tr(a["state_mlstm_n"][0], (1, 2, 0)),
        "state_m": a["state_mlstm_m"][0].T,
        "conv_w": tr(conv_w.reshape(2, 4, 22, 128), (0, 3, 2, 1)),
        "state_conv": tr(a["state_conv"].reshape(2, 8, 2, 22, 128), (0, 4, 3, 2, 1)),
        "w_ukT": tr(a["w_uk"], (2, 1, 0)), "w_uv": tr(a["w_uv"].reshape(2, 128, 1024), (1, 0, 2)),
        "cache_ckv": a["cache_ckv"], "cache_kpe": a["cache_kpe"],
        "page_table": a["page_table"].reshape(1, 64),
        "ident": _np.eye(128, dtype=f32), "reset": reset,
        "cmask": _np.where(j[:, None] <= j[None, :], f32(1e30), f32(-1e30)).astype(f32),
        "amask": _np.where(j[None, :] <= j[:, None], f32(0), f32(-1e30)).astype(f32),
        "cos": _np.cos(ang).astype(f32), "sin": (_np.sin(ang) * sign).astype(f32),
    }
    nc = _bacc.Bacc("TRN2", target_bir_lowering=False, num_devices=1)
    t, feed = {}, {}
    for n, v in arrays.items():
        v = _np.ascontiguousarray(v)
        feed["in_" + n] = v
        t[n] = nc.dram_tensor("in_" + n, v.shape, _mybir.dt.from_np(v.dtype), kind="ExternalInput").ap()
    for n, s in _OUT:
        t[n] = nc.dram_tensor("out_" + n, s, _mybir.dt.float32, kind="ExternalOutput").ap()
    t["row_scratch"] = nc.dram_tensor("row_scratch", (4, 3, 1032), _mybir.dt.float32, kind="Internal").ap()
    t["n_phys"] = a["cache_ckv"].shape[0]
    build(nc, t)
    r = _run(nc, [feed], core_ids=[0]).results[0]
    r = {n: _np.asarray(r["out_" + n]) for n, _ in _OUT}
    y = tr(r["y"], (2, 1, 0)).reshape(1032, 1024)
    ck = tr(r["ckv_out"], (2, 1, 0)).reshape(1032, 256)
    kp = r["kpe_out"].T
    cv = tr(r["conv_out"], (0, 3, 2, 1)).reshape(2, 10, 2816)
    conv_s = _np.stack([tr(r["conv_prev"], (0, 3, 2, 1)).reshape(2, 8, 2816), cv[:, 2:10]], axis=2)
    return (y[None, :1024], y[1024:, None],
            r["C_prompt"][None, None], r["n_prompt"][None, None, :, :, 0], r["m_prompt"][None, None, :, 0],
            cv[:, None, 0:2], ck[None, :1024], kp[None, :1024],
            tr(r["C_sample"], (1, 0, 2, 3))[None], tr(r["n_sample"], (2, 0, 1))[None], r["m_sample"].T[None],
            conv_s, ck[1024:, None], kp[1024:, None])
```
